# Optimizing a Trainium2 kernel written in Bass

```python
import math
import jax
import jax.numpy as jnp
from jax import lax
import numpy as np
import jax, jax.numpy as jnp

D_MODEL = 2048
BATCH = 1
SEQ = 256
DEPTH = 1

D_MIX = D_MODEL
D_POOL = D_MIX // 2
POOL_WINDOWS = (2, 4, 8, 16)
N_POOL_GROUPS = len(POOL_WINDOWS)
POOL_GROUP = D_POOL // N_POOL_GROUPS
D_ATTN = D_MIX - D_POOL
HEAD_DIM = 128
N_HEADS = D_ATTN // HEAD_DIM
IDX_HEADS = 16
IDX_DIM = 64
TOPK_MAX = 256
Q_BLOCK = 128
D_FF = 5632
CONV_WIDTH = 3
EPS = 1e-6

D_IN = D_POOL + 3 * D_ATTN + IDX_HEADS * IDX_DIM + IDX_DIM + IDX_HEADS


def rmsnorm(x, g):
    xf = x.astype(jnp.float32)
    y = xf * lax.rsqrt(jnp.mean(xf * xf, axis=-1, keepdims=True) + EPS)
    return (y * g.astype(jnp.float32)).astype(x.dtype)

def pool_mixer(u, pool_w, pool_scale):
    B, S, C = u.shape
    uf = u.astype(jnp.float32)
    csum = jnp.concatenate([jnp.zeros((B, 1, C), jnp.float32), jnp.cumsum(uf, axis=1)], axis=1)
    t = jnp.arange(S)
    outs = []
    for gi, w in enumerate(POOL_WINDOWS):
        lo = jnp.maximum(t + 1 - w, 0)
        cnt = (t + 1 - lo).astype(jnp.float32)[None, :, None]
        c_g = csum[:, :, gi * POOL_GROUP:(gi + 1) * POOL_GROUP]
        mean = (c_g[:, 1:] - c_g[:, lo]) / cnt
        outs.append(mean - uf[:, :, gi * POOL_GROUP:(gi + 1) * POOL_GROUP])
    d = jnp.stack(outs, axis=2).astype(u.dtype)
    y = jnp.einsum('bsgc,gcd->bsgd', d, pool_w).reshape(B, S, C)
    return y * pool_scale

def dsa_attention(q, k, v, q_idx, k_idx, w_idx):
    B, S, H, Dh = q.shape
    topk = min(TOPK_MAX, S // 4)
    n_blocks = S // Q_BLOCK
    key_pos = jnp.arange(S)
    scale = Dh ** -0.5
    neg = jnp.finfo(jnp.float32).min

    def one_block(blk):
        start = blk * Q_BLOCK
        qb = lax.dynamic_slice_in_dim(q, start, Q_BLOCK, axis=1)
        qib = lax.dynamic_slice_in_dim(q_idx, start, Q_BLOCK, axis=1)
        wb = lax.dynamic_slice_in_dim(w_idx, start, Q_BLOCK, axis=1)
        q_pos = start + jnp.arange(Q_BLOCK)
        rel = jax.nn.relu(jnp.einsum('bthd,bsd->bths', qib.astype(jnp.float32), k_idx.astype(jnp.float32)))
        iscore = jnp.einsum('bths,bth->bts', rel, wb.astype(jnp.float32))
        causal = key_pos[None, :] <= q_pos[:, None]
        iscore = jnp.where(causal[None], iscore, neg)
        _, sel = lax.top_k(iscore, topk)
        valid = sel <= q_pos[None, :, None]
        k_sel = jax.vmap(lambda kb, ib: kb[ib])(k, sel)
        v_sel = jax.vmap(lambda vb, ib: vb[ib])(v, sel)
        s = jnp.einsum('bthd,btjhd->bhtj', qb, k_sel).astype(jnp.float32) * scale
        s = jnp.where(valid[:, None], s, neg)
        p = jax.nn.softmax(s, axis=-1).astype(v.dtype)
        return jnp.einsum('bhtj,btjhd->bthd', p, v_sel)

    out = lax.map(one_block, jnp.arange(n_blocks, dtype=jnp.int32))
    return jnp.transpose(out, (1, 0, 2, 3, 4)).reshape(B, S, H * Dh)

def conv_ffn(h, w_up, conv_w, conv_b, w_down):
    B, S, _ = h.shape
    up = h @ w_up
    up_p = jnp.pad(up, ((0, 0), (CONV_WIDTH - 1, 0), (0, 0)))
    c = conv_b + sum(conv_w[j] * up_p[:, j:j + S] for j in range(CONV_WIDTH))
    gate, val = jnp.split(c, 2, axis=-1)
    return (jax.nn.silu(gate) * val) @ w_down

def first_inputs(seed: int = 0) -> dict:
    key = jax.random.key(seed)
    ks = jax.random.split(key, 14)
    f32 = jnp.float32
    nrm = lambda k, shape, s: jax.random.normal(k, shape, f32) * s
    return {
        "x": nrm(ks[0], (BATCH, SEQ, D_MODEL), 1.0),
        "attn_norm_g": 1.0 + nrm(ks[1], (D_MODEL,), 0.02),
        "w_in": nrm(ks[2], (D_MODEL, D_IN), D_MODEL ** -0.5),
        "pool_w": nrm(ks[3], (N_POOL_GROUPS, POOL_GROUP, POOL_GROUP), POOL_GROUP ** -0.5),
        "pool_scale": 1.0 + nrm(ks[4], (D_POOL,), 0.02),
        "q_norm_g": 1.0 + nrm(ks[5], (HEAD_DIM,), 0.02),
        "k_norm_g": 1.0 + nrm(ks[6], (HEAD_DIM,), 0.02),
        "w_out": nrm(ks[7], (D_MIX, D_MODEL), D_MIX ** -0.5),
        "ffn_norm_g": 1.0 + nrm(ks[8], (D_MODEL,), 0.02),
        "w_up": nrm(ks[9], (D_MODEL, 2 * D_FF), D_MODEL ** -0.5),
        "conv_w": nrm(ks[10], (CONV_WIDTH, 2 * D_FF), CONV_WIDTH ** -0.5),
        "conv_b": nrm(ks[11], (2 * D_FF,), 0.01),
        "w_down": nrm(ks[12], (D_FF, D_MODEL), D_FF ** -0.5),
    }

def first_block(x, attn_norm_g, w_in, pool_w, pool_scale, q_norm_g, k_norm_g, w_out,
              ffn_norm_g, w_up, conv_w, conv_b, w_down):
    B, S, _ = x.shape
    for _layer in range(DEPTH):
        h = rmsnorm(x, attn_norm_g)
        z = h @ w_in
        o = 0
        u_pool = z[..., o:o + D_POOL]; o += D_POOL
        q = z[..., o:o + D_ATTN].reshape(B, S, N_HEADS, HEAD_DIM); o += D_ATTN
        k = z[..., o:o + D_ATTN].reshape(B, S, N_HEADS, HEAD_DIM); o += D_ATTN
        v = z[..., o:o + D_ATTN].reshape(B, S, N_HEADS, HEAD_DIM); o += D_ATTN
        q_idx = z[..., o:o + IDX_HEADS * IDX_DIM].reshape(B, S, IDX_HEADS, IDX_DIM); o += IDX_HEADS * IDX_DIM
        k_idx = z[..., o:o + IDX_DIM]; o += IDX_DIM
        w_idx = z[..., o:o + IDX_HEADS] * (IDX_HEADS ** -0.5) * (IDX_DIM ** -0.5)
        q = rmsnorm(q, q_norm_g)
        k = rmsnorm(k, k_norm_g)
        y_pool = pool_mixer(u_pool, pool_w, pool_scale)
        y_attn = dsa_attention(q, k, v, q_idx, k_idx, w_idx)
        x = x + jnp.concatenate([y_pool, y_attn], axis=-1) @ w_out
        x = x + conv_ffn(rmsnorm(x, ffn_norm_g), w_up, conv_w, conv_b, w_down)
    return x


MOBA_HEADS = 8
MOBA_HEAD_DIM = 128
MOBA_WIDTH = MOBA_HEADS * MOBA_HEAD_DIM
MOBA_BLOCK = 256
MOBA_TOPK = 3
MOBA_Q_CHUNK = 64
PARTIAL_ROPE_DIM = MOBA_HEAD_DIM // 4
MLA_HEADS = 8
MLA_NOPE_DIM = 128
MLA_ROPE_DIM = 64
MLA_V_DIM = 128
MLA_Q_RANK = 512
MLA_KV_RANK = 256
MLA_WIDTH = MLA_HEADS * MLA_V_DIM
MLA_Q_BLOCK = 128
ROPE_THETA = 500000.0
D_FF_2 = -(-8 * D_MODEL // (3 * 256)) * 256
N_BRANCHES = 2
IN_SIZES = (MOBA_WIDTH, MOBA_WIDTH, MOBA_WIDTH, MLA_Q_RANK, MLA_KV_RANK, MLA_ROPE_DIM, N_BRANCHES * D_MODEL)
IN_COLS = sum(IN_SIZES)


def rmsnorm_2(x, g):
    x32 = x.astype(jnp.float32)
    y = x32 * lax.rsqrt(jnp.mean(x32 * x32, axis=-1, keepdims=True) + EPS)
    return (y * g.astype(jnp.float32)).astype(x.dtype)

def rope(x, positions):
    d = x.shape[-1]
    inv_freq = ROPE_THETA ** (-jnp.arange(0, d, 2, dtype=jnp.float32) / d)
    ang = positions.astype(jnp.float32)[..., None] * inv_freq
    cos = jnp.cos(ang)[:, :, None, :]
    sin = jnp.sin(ang)[:, :, None, :]
    x32 = x.astype(jnp.float32)
    x1, x2 = x32[..., : d // 2], x32[..., d // 2:]
    out = jnp.concatenate([x1 * cos - x2 * sin, x2 * cos + x1 * sin], axis=-1)
    return out.astype(x.dtype)

def moba_attention(q, k, v):
    B, S, H, Dh = q.shape
    nb = -(-S // MOBA_BLOCK)
    n_sel = min(MOBA_TOPK, nb)
    pad = nb * MOBA_BLOCK - S
    kp = jnp.pad(k, ((0, 0), (0, pad), (0, 0), (0, 0)))
    vp = jnp.pad(v, ((0, 0), (0, pad), (0, 0), (0, 0)))
    kb = kp.reshape(B, nb, MOBA_BLOCK, H, Dh).transpose(0, 3, 1, 2, 4)
    vb = vp.reshape(B, nb, MOBA_BLOCK, H, Dh).transpose(0, 3, 1, 2, 4)
    k_mean = jnp.mean(kb.astype(jnp.float32), axis=3)
    scale = Dh ** -0.5
    bidx = jnp.arange(B)[:, None, None, None]
    hidx = jnp.arange(H)[None, None, :, None]

    def chunk(c):
        start = c * MOBA_Q_CHUNK
        qc = lax.dynamic_slice_in_dim(q, start, MOBA_Q_CHUNK, axis=1)
        blk = start // MOBA_BLOCK
        qpos = start + jnp.arange(MOBA_Q_CHUNK)
        gate = jnp.einsum('bqhd,bhnd->bqhn', qc.astype(jnp.float32), k_mean)
        past = jnp.arange(nb) < blk
        gate = jnp.where(past[None, None, None, :], gate, -jnp.inf)
        _, sel = lax.top_k(gate, n_sel)
        sel_valid = jnp.arange(n_sel) < blk
        k_sel = kb[bidx, hidx, sel]
        v_sel = vb[bidx, hidx, sel]
        s_sel = jnp.einsum('bqhd,bqhkjd->bqhkj', qc, k_sel).astype(jnp.float32) * scale
        s_sel = jnp.where(sel_valid[None, None, None, :, None], s_sel, -jnp.inf)
        s_sel = s_sel.reshape(B, MOBA_Q_CHUNK, H, n_sel * MOBA_BLOCK)
        k_own = lax.dynamic_slice_in_dim(kp, blk * MOBA_BLOCK, MOBA_BLOCK, axis=1)
        v_own = lax.dynamic_slice_in_dim(vp, blk * MOBA_BLOCK, MOBA_BLOCK, axis=1)
        s_own = jnp.einsum('bqhd,bjhd->bqhj', qc, k_own).astype(jnp.float32) * scale
        kpos = blk * MOBA_BLOCK + jnp.arange(MOBA_BLOCK)
        causal = kpos[None, :] <= qpos[:, None]
        s_own = jnp.where(causal[None, :, None, :], s_own, -jnp.inf)
        p = jax.nn.softmax(jnp.concatenate([s_sel, s_own], axis=-1), axis=-1).astype(v.dtype)
        p_sel = p[..., : n_sel * MOBA_BLOCK].reshape(B, MOBA_Q_CHUNK, H, n_sel, MOBA_BLOCK)
        p_own = p[..., n_sel * MOBA_BLOCK:]
        return (jnp.einsum('bqhkj,bqhkjd->bqhd', p_sel, v_sel)
                + jnp.einsum('bqhj,bjhd->bqhd', p_own, v_own))

    outs = lax.map(chunk, jnp.arange(S // MOBA_Q_CHUNK))
    return outs.transpose(1, 0, 2, 3, 4).reshape(B, S, H, Dh)

def mla_attention(q_nope, q_rope, k_nope, k_rope, v):
    B, S, H, _ = q_nope.shape
    scale = (MLA_NOPE_DIM + MLA_ROPE_DIM) ** -0.5
    kpos = jnp.arange(S)

    def block(c):
        start = c * MLA_Q_BLOCK
        qn = lax.dynamic_slice_in_dim(q_nope, start, MLA_Q_BLOCK, axis=1)
        qr = lax.dynamic_slice_in_dim(q_rope, start, MLA_Q_BLOCK, axis=1)
        s = (jnp.einsum('bqhd,bkhd->bhqk', qn, k_nope)
             + jnp.einsum('bqhd,bkd->bhqk', qr, k_rope)).astype(jnp.float32) * scale
        qpos = start + jnp.arange(MLA_Q_BLOCK)
        s = jnp.where((kpos[None, :] <= qpos[:, None])[None, None], s, -jnp.inf)
        p = jax.nn.softmax(s, axis=-1).astype(v.dtype)
        return jnp.einsum('bhqk,bkhd->bqhd', p, v)

    outs = lax.map(block, jnp.arange(S // MLA_Q_BLOCK))
    return outs.transpose(1, 0, 2, 3, 4).reshape(B, S, H * MLA_V_DIM)

def second_inputs(seed: int = 0) -> dict:
    key = jax.random.key(seed)
    ks = jax.random.split(key, 17)

    def dense(k, shape, fan_in):
        return jax.random.normal(k, shape, jnp.float32) * (fan_in ** -0.5)

    def gain(k, shape):
        return 1.0 + 0.02 * jax.random.normal(k, shape, jnp.float32)

    L = DEPTH
    return {
        "x": jax.random.normal(ks[0], (BATCH, SEQ, D_MODEL), jnp.float32),
        "positions": jnp.broadcast_to(jnp.arange(SEQ, dtype=jnp.int32), (BATCH, SEQ)),
        "attn_norm": gain(ks[1], (L, D_MODEL)),
        "w_in": dense(ks[2], (L, D_MODEL, IN_COLS), D_MODEL),
        "q_norm": gain(ks[3], (L, MLA_Q_RANK)),
        "w_uq": dense(ks[4], (L, MLA_Q_RANK, MLA_HEADS * (MLA_NOPE_DIM + MLA_ROPE_DIM)), MLA_Q_RANK),
        "kv_norm": gain(ks[5], (L, MLA_KV_RANK)),
        "w_ukv": dense(ks[6], (L, MLA_KV_RANK, MLA_HEADS * (MLA_NOPE_DIM + MLA_V_DIM)), MLA_KV_RANK),
        "w_branch_a": dense(ks[7], (L, MOBA_WIDTH, D_MODEL), MOBA_WIDTH),
        "w_branch_b": dense(ks[8], (L, MLA_WIDTH, D_MODEL), MLA_WIDTH),
        "w_out": dense(ks[9], (L, D_MODEL, D_MODEL), D_MODEL),
        "ffn_norm": gain(ks[10], (L, D_MODEL)),
        "w_gate": dense(ks[11], (L, D_MODEL, D_FF_2), D_MODEL),
        "w_up": dense(ks[12], (L, D_MODEL, D_FF_2), D_MODEL),
        "w_down": dense(ks[13], (L, D_FF_2, D_MODEL), D_FF_2),
        "final_norm": gain(ks[14], (D_MODEL,)),
    }

def second_block(x, positions, attn_norm, w_in, q_norm, w_uq, kv_norm, w_ukv, w_branch_a, w_branch_b,
              w_out, ffn_norm, w_gate, w_up, w_down, final_norm):
    B, S, _ = x.shape
    split_at = np.cumsum(np.array(IN_SIZES))[:-1].tolist()
    h = x
    for l in range(DEPTH):
        xn = rmsnorm_2(h, attn_norm[l])
        proj = xn @ w_in[l]
        q_a, k_a, v_a, c_q, c_kv, k_r, gates = jnp.split(proj, split_at, axis=-1)

        q_a = q_a.reshape(B, S, MOBA_HEADS, MOBA_HEAD_DIM)
        k_a = k_a.reshape(B, S, MOBA_HEADS, MOBA_HEAD_DIM)
        v_a = v_a.reshape(B, S, MOBA_HEADS, MOBA_HEAD_DIM)
        q_a = jnp.concatenate([rope(q_a[..., :PARTIAL_ROPE_DIM], positions), q_a[..., PARTIAL_ROPE_DIM:]], axis=-1)
        k_a = jnp.concatenate([rope(k_a[..., :PARTIAL_ROPE_DIM], positions), k_a[..., PARTIAL_ROPE_DIM:]], axis=-1)
        y_a = moba_attention(q_a, k_a, v_a).reshape(B, S, MOBA_WIDTH)

        qh = (rmsnorm_2(c_q, q_norm[l]) @ w_uq[l]).reshape(B, S, MLA_HEADS, MLA_NOPE_DIM + MLA_ROPE_DIM)
        q_nope, q_rope = qh[..., :MLA_NOPE_DIM], rope(qh[..., MLA_NOPE_DIM:], positions)
        kv = (rmsnorm_2(c_kv, kv_norm[l]) @ w_ukv[l]).reshape(B, S, MLA_HEADS, MLA_NOPE_DIM + MLA_V_DIM)
        k_nope, v_b = kv[..., :MLA_NOPE_DIM], kv[..., MLA_NOPE_DIM:]
        k_rope = rope(k_r[:, :, None, :], positions)[:, :, 0, :]
        y_b = mla_attention(q_nope, q_rope, k_nope, k_rope, v_b)

        g = jax.nn.sigmoid(gates.astype(jnp.float32)).astype(x.dtype)
        g_a, g_b = g[..., :D_MODEL], g[..., D_MODEL:]
        mixed = g_a * (y_a @ w_branch_a[l]) + g_b * (y_b @ w_branch_b[l])
        h = h + mixed @ w_out[l]

        hn = rmsnorm_2(h, ffn_norm[l])
        h = h + (jax.nn.silu(hn @ w_gate[l]) * (hn @ w_up[l])) @ w_down[l]
    return rmsnorm_2(h, final_norm)


def setup_inputs(seed=0):
    out = dict(first_inputs(seed))
    for name, value in second_inputs(seed + 1).items():
        if name != "x":
            out[name + "_2"] = value
    return out


def reference(
    x, attn_norm_g, w_in, pool_w, pool_scale, q_norm_g, k_norm_g, w_out, ffn_norm_g, w_up,
    conv_w, conv_b, w_down, positions_2, attn_norm_2, w_in_2, q_norm_2, w_uq_2, kv_norm_2,
    w_ukv_2, w_branch_a_2, w_branch_b_2, w_out_2, ffn_norm_2, w_gate_2, w_up_2, w_down_2,
    final_norm_2,
):
    x = first_block(
        x, attn_norm_g, w_in, pool_w, pool_scale, q_norm_g, k_norm_g, w_out, ffn_norm_g, w_up,
        conv_w, conv_b, w_down,
    )
    return second_block(
        x, positions_2, attn_norm_2, w_in_2, q_norm_2, w_uq_2, kv_norm_2, w_ukv_2, w_branch_a_2,
        w_branch_b_2, w_out_2, ffn_norm_2, w_gate_2, w_up_2, w_down_2, final_norm_2,
    )


_drawn_inputs = setup_inputs


def setup_inputs(seed=0):
    import zlib

    import numpy as np

    out = dict(_drawn_inputs(seed))
    spreads = {}
    factors = {'pool_scale': 4.567,
     'q_norm_g': 8.0,
     'k_norm_g': 8.0,
     'ffn_norm_g': 3.956,
     'conv_b': 7.842,
     'attn_norm_2': 8.0,
     'q_norm_2': 8.0,
     'kv_norm_2': 8.0,
     'ffn_norm_2': 4.745,
     'final_norm_2': 2.813}
    for name, (base, spread) in spreads.items():
        noise = np.random.default_rng([zlib.crc32(name.encode()), seed]).standard_normal(out[name].shape)
        drawn = base * np.exp(spread * noise) if base else spread * noise
        out[name] = jnp.asarray(drawn.astype(out[name].dtype))
    for name, factor in factors.items():
        out[name] = (out[name] * factor).astype(out[name].dtype)
    return out
```

```python
import concourse.bass as bass
from concourse import mybir
from contextlib import ExitStack
import math
import numpy as np

F32 = mybir.dt.float32
F32R = mybir.dt.float32r
I32 = mybir.dt.int32
ALU = mybir.AluOpType
ACT = mybir.ActivationFunctionType
AX = mybir.AxisListType

P = 128
S = 256
NT = S // P
D = 2048
KT = D // P
CW = 512
KC = 2
RING = 4
LEAD = 3
DFF = 5632
FT = DFF // P
PAIRS = DFF // CW
HD = 128
NH = 8
TOPK = 64
IDX_HEADS, IDX_DIM = 16, 64
WINDOWS = (2, 4, 8, 16)
ROPE_A, ROPE_B = 32, 64
EPS = 1e-6
FMIN = -3.4028234663852886e38
ROPE_THETA = 500000.0
ROUND = 1.5 * 2.0 ** 23
TWO_PI = (6.28125, 1.93500518798828125e-3, 3.019915981956753e-07)
BIG = 3.3e38
KEYS = P + S

G_ATTN1, G_FFN1, G_ATTN2, G_FFN2, G_POOL, G_CQ, G_CKV, G_Q, G_K = 0, 16, 32, 48, 64, 72, 76, 78, 79
G_ROWS = 80
CONV_COL = G_ROWS
CT = 2 * DFF // P


def rel_unit(u):
    return (0, 8 * u, 8, P) if u < 2 else (1, 4 * (u - 2), 4, S)


def plan():
    groups, first, at = [], [], {}

    def group(*g):
        first.append(first[-1] + len(groups[-1][3]) if groups else 0)
        groups.append(g)
        return first[-1] + len(g[3])

    def put(n, *step):
        at.setdefault(n, []).append(step)

    whole = list(range(KT // KC))

    def copy_out(n, kind, *dest):
        put(n, "evac", kind, len(groups) - 1, *dest)
        if kind == "stage" and dest[0] in ("q1", "k1"):
            put(n + 1, "headsq", dest[0], len(groups) - 1)
            put(n + 3, "headscale", dest[0], len(groups) - 1)
            put(n + 4, "turn_copy", dest[0], len(groups) - 1)
            put(n + 5, "copy2", *dest)
        elif kind == "stage" and dest[0] in ("qa", "ka"):
            put(n + 1, "rope", "a", len(groups) - 1)
            put(n + 4, "turn_copy", dest[0], len(groups) - 1)
            put(n + 5, "copy2", *dest)
        elif kind == "stage" and dest[0] == "qr":
            put(n + 1, "rope", "b", len(groups) - 1)
            put(n + 4, "turn_copy", dest[0], len(groups) - 1)
            put(n + 5, "copy2", *dest)
        elif kind == "stage":
            put(n + 1, "turn_copy", dest[0], len(groups) - 1)
            put(n + 2, "copy2", *dest)

    def attend(a, which, pair):
        put(a, "scores", which, pair)
        put(a + 1, "mask", which)
        put(a + 2, "exp", which)
        put(a + 3, "norm", which)
        put(a + 4, "turn_p", which)
        put(a + 5, "copy_p", which)
        put(a + 6, "pv", which, pair)
        put(a + 7, "split_y", which, pair)

    def residual(n, g, b, gain):
        put(b, "res", g, n)
        put(b + 1, "square", g, n)
        if gain is not None:
            put(b + 1, "turn_x", n, g)
            put(b + 2, "split_x", n, gain, 0)
            put(b + 3, "split_x", n, gain, 1)
        if n == 3:
            put(b + 3, "rstd")

    b = group("w_in", 5120, 80, whole, "x")
    put(b, "evac_kw", 0); put(b + 1, "turn_ki"); put(b + 2, "copy_ki")
    for n in range(2):
        b = group("w_in", 4096 + CW * n, CW, whole, "x")
        copy_out(b, "stage", "qi", n)
    for u in range(6):
        put(27 + 2 * u, "rel", u); put(28 + 2 * u, "relu", u); put(28 + 2 * u, "isc", u)
    for half in range(2):
        for name, col in (("q1", 1024), ("k1", 2048), ("v1", 3072)):
            b = group("w_in", col + CW * half, CW, whole, "x")
            copy_out(b, "v" if name == "v1" else "stage", name, half)
            if name == "q1" and half == 0:
                for r in range(TOPK // 8):
                    put(b + 8 + r, "topk", r)
                put(b + 16, "select")
    attend(50, "one", 0); attend(58, "one", 1)
    attend(73, "one", 2); attend(81, "one", 3)
    for n in range(2):
        b = group("w_in", CW * n, CW, whole, "x")
        put(b, "evac", "stage", len(groups) - 1)
        put(b + 1, "pool_d", n, len(groups) - 1); put(b + 2, "copy_d", n)
        put(b + 3, "pool_y", n); put(b + 4, "split_pool", n)
    for n in range(4):
        b = group("w_out", CW * n, CW, [0, 1, 4, 5, 6, 7, 2, 3] if n == 0 else whole, "y")
        residual(n, len(groups) - 1, b, G_FFN1)
    up1 = b
    for j in range(PAIRS):
        group("w_up", CW * j, CW, whole, "x")
        b = group("w_up", DFF + CW * j, CW, whole, "x")
    for n in range(4):
        b = group("w_down", CW * n, CW, list(range(FT // KC)), "f")
        residual(n, len(groups) - 1, b, G_ATTN2)
    b = group("w_in_2", 3072, 512, whole, "x")
    put(b, "evac", "stage", len(groups) - 1); put(b + 1, "lat_square", "cq", len(groups) - 1)
    put(b + 1, "turn_lat", "cq", len(groups) - 1)
    put(b + 2, "split_lat", "cq"); put(b + 2, "lat_rstd", "cq")
    b = group("w_in_2", 3584, 320, whole, "x")
    put(b, "evac", "ckv", len(groups) - 1); put(b + 1, "lat_square", "ckv", len(groups) - 1)
    put(b + 1, "turn_lat", "ckv", len(groups) - 1)
    put(b + 2, "split_lat", "ckv"); put(b + 2, "lat_rstd", "ckv"); put(b + 1, "rope", "kr", len(groups) - 1)
    put(b + 4, "turn_kr"); put(b + 5, "copy_kr")
    for name, col in (("qa", 0), ("ka", 1024), ("va", 2048)):
        b = group("w_in_2", col, CW, whole, "x")
        copy_out(b, "va" if name == "va" else "stage", name, 0)
    attend(b + 1, "moba", 0); attend(b + 9, "moba", 1)
    for n in range(3):
        b = group("w_uq_2", n, CW, [0, 1], "cq")
        copy_out(b, "stage", "qr" if n == 2 else "qn", n)
    for name, col in (("qa", 0), ("ka", 1024), ("va", 2048)):
        b = group("w_in_2", col + CW, CW, whole, "x")
        copy_out(b, "va" if name == "va" else "stage", name, 1)
    gates = [(0, 0), (1, 0), (0, 1), (1, 1), (0, 2), (1, 2), (0, 3), (1, 3)]
    for k, (ab, n) in enumerate(gates):
        if k < 4:
            b = group("w_ukv_2", CW * k, CW, [0], "ckv")
            put(b, "evac", "ukv", len(groups) - 1, k); put(b + 1, "turn_kn", k, len(groups) - 1)
            put(b + 2, "copy_kn", k)
            attend(b + 3, "mla", k)
        elif k < 6:
            attend(b + 3, "moba", k - 2)
        b = group("w_in_2", 3904 + ab * D + CW * n, CW, whole, "x")
        put(b, "evac", "gate", len(groups) - 1, ab, n)
    for n in range(4):
        b = group("w_branch_a_2", CW * n, CW, [0, 1, 2, 3], "ya")
        put(b, "sigmoid", n); put(b, "mix_a", n, len(groups) - 1)
        b = group("w_branch_b_2", CW * n, CW, [0, 1, 2, 3], "yb")
        put(b, "mix_b", n, len(groups) - 1); put(b + 1, "turn_mix", len(groups) - 1); put(b + 2, "split_mix", n)
    for n in range(4):
        b = group("w_out_2", CW * n, CW, whole, "m")
        residual(n, len(groups) - 1, b, G_FFN2)
    up2 = b
    for j in range(PAIRS):
        group("w_gate_2", CW * j, CW, whole, "x")
        b = group("w_up_2", CW * j, CW, whole, "x")
    for n in range(4):
        b = group("w_down_2", CW * n, CW, list(range(FT // KC)), "f")
        residual(n, len(groups) - 1, b, None)
    return groups, first, at, up1, up2, b


class Count:

    def __init__(self):
        self.now, self.i, self.per = 0, None, 0

    def value(self, more=0):
        return self.now + more + (self.i * self.per if self.per else 0)

    def sixteens(self):
        return 16 * self.now + (self.i * (16 * self.per) if self.per else 0)

    def turns(self, ring, more=0):
        assert self.per % ring == 0
        return (self.now + more) // ring + (self.i * (self.per // ring) if self.per else 0)


def two_layer_kernel(nc, a, out):
    groups, first, at, up1, up2, n_end = plan()
    G_UP1 = first.index(up1)
    G_UP2 = first.index(up2)
    G_IN2 = [g[0] for g in groups].index("w_in_2")
    gate_groups = [g for g, v in enumerate(groups) if v[0] == "w_in_2" and v[1] >= 3904]
    ctx = ExitStack()
    with ctx:
        def sb(name, shape, dt=F32, c=ctx):
            return c.enter_context(nc.sbuf_tensor(name, shape, dt))

        def sem(name):
            return ctx.enter_context(nc.semaphore(name))

        x = sb("x_res", [P, NT, D])
        xT_hi, xT_lo = sb("xT_hi", [P, KT, S], F32R), sb("xT_lo", [P, KT, S], F32R)
        w_raw = sb("w_raw", [P, RING, KC, CW])
        w_hi, w_lo = sb("w_hi", [P, RING, KC, CW], F32R), sb("w_lo", [P, RING, KC, CW], F32R)
        stage = sb("stage", [P, 2, NT, CW])
        half_a, half_b = sb("half_a", [P, 4, S]), sb("half_b", [P, 4, S])
        ident = sb("ident", [P, P])
        causal = sb("causal", [P, KEYS])
        cols = sb("cols", [P, G_ROWS + 4 * CT])
        gqk = sb("gqk", [P, 1])
        cos, sin = sb("cos", [P, NT, 48]), sb("sin", [P, NT, 48])
        sumsq, meansq, rstd = sb("sumsq", [P, NT, 4]), sb("meansq", [P, NT]), sb("rstd", [P, NT])
        pos_i, pos_f = sb("pos_i", [P, NT], I32), sb("pos_f", [P, NT])
        minus_half = sb("minus_half", [P, 8])
        hsum, hmean, hrstd = sb("hsum", [P, NT, 4]), sb("hmean", [P, NT, 4]), sb("hrstd", [P, NT, 4])
        lsum, lmean = sb("lsum", [P, 2, NT]), sb("lmean", [P, 2, NT])
        lrstd = sb("lrstd", [P, 2, NT])
        negmax, psum_, pinv = sb("negmax", [P, 4]), sb("p_sum", [P, 4]), sb("p_inv", [P, 4])
        with ExitStack() as r:
            y_hi, y_lo = sb("y_hi", [P, KT, S], F32R, r), sb("y_lo", [P, KT, S], F32R, r)
            with ExitStack() as q:
                q1T, k1T = sb("q1T", [P, NH, S], F32, q), sb("k1T", [P, NH, S], F32, q)
                v1 = sb("v1", [P, NT, NH * HD], F32, q)
                with ExitStack() as s:
                    qiT = sb("qiT", [P, IDX_HEADS // 2, S], F32, s)
                pool_w = sb("pool_w", [P, 4, 2, S], F32, q)
                kiT = sb("kiT", [P, S], F32, q)
                kdup = sb("kdup", [P, NT, P], F32, q)
                widx = sb("widx", [P, NT, IDX_HEADS], F32, q)
                isc = sb("isc", [P, KEYS], F32, q)
                picked = sb("picked", [P, 2, KEYS], F32, q)
                top8 = sb("top8", [P, 2, 8], F32, q)
                sel = sb("sel", [P, KEYS], F32, q)
                hsq = sb("hsq", [P, CW], F32, q)
                pool_m = sb("pool_m", [P, 4, KEYS], F32, q)
                dT = sb("dT", [P, 4, S], F32, q)
            with ExitStack() as q:
                with ExitStack() as s:
                    gate = sb("gate", [P, 4, 2, NT, CW], F32, s)
                with ExitStack() as s:
                    m_hl = sb("m_hl", [P, 4, 2, 4, S], F32R, s)
                with ExitStack() as s:
                    krd = sb("krd", [P, NT, P], F32, s)
                    sb("over_gate0", [P, 2 * NT * CW - NT * P], F32, s)
                    cqT = sb("cqT", [P, 2, 4, S], F32R, s)
                    qnT = sb("qnT", [P, NH, S], F32, s)
                    qrT = sb("qrT", [P, NH // 2, S], F32, s)
                    ckvT = sb("ckvT", [P, 2, 2, S], F32R, s)
                sb("all_gates", [P, 4, 2, NT, CW], F32, q)
                qaT, kaT = sb("qaT", [P, 4, S], F32, q), sb("kaT", [P, 4, S], F32, q)
                va = sb("va", [P, NT, CW], F32, q)
                knT = sb("knT", [P, 2, 2, S], F32, q)
                vb = sb("vb", [P, 2, NT, 2 * HD], F32, q)
                krT = sb("krT", [P, 2, S], F32, q)
                rtmp = sb("rtmp", [P, 2, CW], F32, q)
        with ExitStack() as r:
            f_hi, f_lo = sb("f_hi", [P, FT, S], F32R, r), sb("f_lo", [P, FT, S], F32R, r)
        rows = stage[:, 0].rearrange("p a b -> p (a b)")
        junk = half_b[:].rearrange("p a b -> p (a b)")
        pbuf = half_a[:].rearrange("p a b -> p (a b)")[:, 0:2 * KEYS]
        pT = half_b[:].rearrange("p a b -> p (a b)")[:, 0:2 * KEYS]
        rel = half_a[:].rearrange("p a b -> p (a b)")
        fgain = w_raw[:].rearrange("p a b c -> p (a b c)")[:, 0:D]

        acc = [[ctx.enter_context(nc.psum_tensor(f"acc{g}{t}", [P, CW], F32)) for t in range(NT)] for g in range(2)]
        T = [ctx.enter_context(nc.psum_tensor(f"bank{b}", [P, CW], F32)) for b in range(4)]

        w_loaded = [sem(f"w_loaded{i}") for i in range(RING)]
        w_split_hi, w_split_lo, w_used = sem("w_split_hi"), sem("w_split_lo"), sem("w_used")
        acc_taken = [sem("acc_taken0"), sem("acc_taken1")]
        x_loaded, const_loaded, rows_loaded, pool_loaded = sem("x_loaded"), sem("const_loaded"), sem("rows_loaded"), sem("pool_loaded")
        fgain_loaded, stored = sem("fgain_loaded"), sem("stored")
        cols_turned, cols_ready, angles, tables = sem("cols_turned"), sem("cols_ready"), sem("angles"), sem("tables")
        consts_set, squared, mean_ready, rstd_ready = sem("consts_set"), sem("squared"), sem("mean_ready"), sem("rstd_ready")
        split_full, split_hi, split_lo = sem("split_full"), sem("split_hi"), sem("split_lo")
        copy_full, copy_done = sem("copy_full"), sem("copy_done")
        heads_mean, heads_rstd, heads_scaled, roped = sem("heads_mean"), sem("heads_rstd"), sem("heads_scaled"), sem("roped")
        rel_full, rel_done, isc_added = sem("rel_full"), sem("rel_done"), sem("isc_added")
        scores_full, scores_masked, exp_done, p_ready = sem("scores_full"), sem("scores_masked"), sem("exp_done"), sem("p_ready")
        lat_squared, lat_mean, lat_rstd = sem("lat_squared"), sem("lat_mean"), sem("lat_rstd")
        gates_open, mixed, kr_zeroed = sem("gates_open"), sem("mixed"), sem("kr_zeroed")
        conv_full, conv_seeded, conv_done, silu_done = sem("conv_full"), sem("conv_seeded"), sem("conv_done"), sem("silu_done")
        hidden, hidden_hi, f_ready = sem("hidden"), sem("hidden_hi"), sem("f_ready")
        dve_step, pool_step, normalised = sem("dve_step"), sem("pool_step"), sem("normalised")

        block = ctx.enter_context(nc.Block())

        def weight_view(name, col, width, c):
            w = a[name]
            if name == "w_uq_2":
                v = w.rearrange("(c k p) (h e) -> c p k h e", p=P, k=KC, e=HD + ROPE_B)[c]
                if col < 2:
                    return [v[:, k, 4 * col:4 * col + 4, 0:HD] for k in range(KC)]
                return [v[:, k, :, HD:HD + ROPE_B] for k in range(KC)]
            v = w.rearrange("(c k p) n -> c p k n", p=P, k=KC)[c]
            return [v[:, :, bass.ds(col, width)]]

        def with_loop(eng, counts, body, per):
            body(0)
            start = {k: c.now for k, c in counts.items()}
            with eng.Fori(1, PAIRS) as j:
                for k, c in counts.items():
                    c.now, c.i, c.per = start[k] - per[k], j, per[k]
                body(j)
                for k, c in counts.items():
                    assert c.now == start[k], (k, c.now, start[k], per[k])
            for k, c in counts.items():
                c.now, c.i, c.per = start[k] + per[k] * (PAIRS - 1), None, 0

        @block.sync
        def _(sp):
            chunk, loads = Count(), [Count() for _ in range(RING)]
            sp.dma_start(x[:, 0], a["x"][0, 0:P, :]).then_inc(x_loaded, 16)
            sp.dma_start(x[:, 1], a["x"][0, P:S, :]).then_inc(x_loaded, 16)

            def load(name, col, width, c):
                if chunk.now >= RING:
                    sp.wait_ge(w_split_lo, chunk.value(1 - RING))
                slot = chunk.now % RING
                views = weight_view(name, col, width, c)
                for k, v in enumerate(views):
                    if len(views) > 1:
                        d = w_raw[:, slot, k, 0:width]
                        d = d.rearrange("p (h e) -> p h e", h=v.shape[1])
                    else:
                        d = w_raw[:, slot, :, 0:width]
                    sp.dma_start(d, v).then_inc(w_loaded[slot], 16)
                chunk.now += 1

            def pair(j, wa, ca, wb, cb):
                for w, c0 in ((wa, ca), (wb, cb)):
                    for c in range(KT // KC):
                        load(w, j * CW + c0, CW, c)

            g = 0
            while g < len(groups):
                if g == G_UP1:
                    with_loop(sp, {"chunk": chunk}, lambda j: pair(j, "w_up", 0, "w_up", DFF), {"chunk": 16})
                    g += 2 * PAIRS
                elif g == G_UP2:
                    with_loop(sp, {"chunk": chunk}, lambda j: pair(j, "w_gate_2", 0, "w_up_2", 0), {"chunk": 16})
                    g += 2 * PAIRS
                else:
                    name, col, width, ks, _ = groups[g]
                    for c in ks:
                        load(name, col, width, c)
                    g += 1
            sp.wait_ge(w_split_lo, chunk.now)
            sp.dma_start(fgain, a["final_norm_2"].rearrange("(a n) -> a n", a=1).to_broadcast([P, D])).then_inc(fgain_loaded, 16)
            for t in range(NT):
                for h in range(2):
                    sp.wait_ge(normalised, 2 * t + h + 1)
                    sp.dma_start(out[0, t * P:(t + 1) * P, h * 1024:(h + 1) * 1024],
                                 x[:, t, h * 1024:(h + 1) * 1024]).then_inc(stored, 16)
            sp.wait_ge(stored, 16 * 2 * NT)

        @block.gpsimd
        def _(pool):
            def rows_of(v, n):
                return v.rearrange("(r p) -> r p", p=P)
            for name, r, n in (("attn_norm_g", G_ATTN1, 16), ("ffn_norm_g", G_FFN1, 16),
                               ("attn_norm_2", G_ATTN2, 16), ("ffn_norm_2", G_FFN2, 16),
                               ("pool_scale", G_POOL, 8), ("q_norm_2", G_CQ, 4), ("kv_norm_2", G_CKV, 2),
                               ("q_norm_g", G_Q, 1), ("k_norm_g", G_K, 1)):
                pool.dma_start(rows[r:r + n, 0:P], rows_of(a[name], n)).then_inc(rows_loaded, 16)
            for k in range(3):
                pool.dma_start(rows[0:CT, (k + 1) * P:(k + 2) * P], rows_of(a["conv_w"][k, :], CT)).then_inc(rows_loaded, 16)
            pool.dma_start(rows[0:CT, 4 * P:5 * P], rows_of(a["conv_b"], CT)).then_inc(rows_loaded, 16)
            pool.dma_start(ident[:], a["c_ident"]).then_inc(const_loaded, 16)
            pool.dma_start(causal[:], a["c_causal"]).then_inc(const_loaded, 16)
            pool.dma_start(pool_m[:], a["c_pool"]).then_inc(const_loaded, 16)
            pool.dma_start(cos[:, 0, :], a["c_freq"]).then_inc(const_loaded, 16)
            pool.dma_start(pos_i[:], a["positions_2"][0, :].rearrange("(t p) -> p t", p=P), allow_slow_non_contiguous=True).then_inc(const_loaded, 16)
            n_rstd, n_heads, n_roped, n_lat, steps = [0], [0], [0], [0], [0]

            def step(ins):
                steps[0] += 1
                ins.then_inc(pool_step, 1)

            def power(n):
                pool.wait_ge(mean_ready, n + 1)
                pool.tensor_tensor(rstd[:], meansq[:], minus_half[:, 0:NT], ALU.pow).then_inc(rstd_ready, 1)
            pool.wait_ge(consts_set, 1)
            power(0)

            def on_heads(kind, g):
                n_heads[0] += 1
                pool.wait_ge(heads_mean, n_heads[0])
                pool.tensor_tensor(hrstd[:].rearrange("p a b -> p (a b)"), hmean[:].rearrange("p a b -> p (a b)"),
                                   minus_half[:], ALU.pow).then_inc(heads_rstd, 1)

            def on_rstd():
                n_rstd[0] += 1
                power(n_rstd[0])

            def on_lat(kind):
                k = ("cq", "ckv").index(kind)
                n_lat[0] += 1
                pool.wait_ge(lat_mean, n_lat[0])
                pool.tensor_tensor(lrstd[:, k], lmean[:, k], minus_half[:, 0:NT], ALU.pow).then_inc(lat_rstd, 1)

            def on_rope(kind, g):
                pool.wait_ge(acc_taken[g % 2], 2 * (g // 2 + 1))
                pool.wait_ge(tables, 2)
                for t in range(NT):
                    st = stage[:, g % 2, t]
                    if kind == "a":
                        half, nh = ROPE_A // 2, 4
                        src = st.rearrange("p (h e) -> p h e", e=HD)[:, :, 0:ROPE_A]
                        f0 = 0
                    else:
                        half, nh = ROPE_B // 2, (1 if kind == "kr" else NH)
                        src = (st[:, 256:320] if kind == "kr" else st).rearrange("p (h e) -> p h e", e=ROPE_B)
                        f0 = 16
                    x1, x2 = src[:, :, 0:half], src[:, :, half:2 * half]
                    cs = cos[:, t, f0:f0 + half].unsqueeze(1).to_broadcast([P, nh, half])
                    sn = sin[:, t, f0:f0 + half].unsqueeze(1).to_broadcast([P, nh, half])
                    m = nh * half
                    tmp = [rtmp[:, k // 2, (k % 2) * 256:(k % 2) * 256 + m].rearrange("p (h e) -> p h e", h=nh) for k in range(4)]
                    if steps[0]:
                        pool.wait_ge(pool_step, steps[0])
                    step(pool.tensor_tensor(tmp[0], x1, cs, ALU.mult))
                    step(pool.tensor_tensor(tmp[1], x2, sn, ALU.mult))
                    step(pool.tensor_tensor(tmp[2], x2, cs, ALU.mult))
                    step(pool.tensor_tensor(tmp[3], x1, sn, ALU.mult))
                    pool.wait_ge(pool_step, steps[0])
                    if kind == "kr":
                        for d in range(2):
                            o1 = krd[:, t, d * 64:d * 64 + 32].unsqueeze(1)
                            o2 = krd[:, t, d * 64 + 32:d * 64 + 64].unsqueeze(1)
                            step(pool.tensor_tensor(o1, tmp[0], tmp[1], ALU.subtract))
                            step(pool.tensor_tensor(o2, tmp[2], tmp[3], ALU.add))
                    else:
                        step(pool.tensor_tensor(x1, tmp[0], tmp[1], ALU.subtract))
                        step(pool.tensor_tensor(x2, tmp[2], tmp[3], ALU.add))
                n_roped[0] += 1
                pool.wait_ge(pool_step, steps[0])
                pool.sem_inc(roped, 1)

            mine = {"headsq": on_heads, "rstd": on_rstd, "lat_rstd": on_lat, "rope": on_rope}
            for n in range(n_end + 8):
                for step_, *args in at.get(n, []):
                    if step_ == "isc" and args[0] == 5:
                        pool.wait_ge(rel_full, 6)
                        pool.dma_start(pool_w[:], a["pool_w"].rearrange("w (k p) d -> p w k d", p=P)).then_inc(pool_loaded, 16)
                    if step_ in mine:
                        mine[step_](*args)

        @block.tensor
        def _(pe):
            chunk, group, splits, copies = Count(), Count(), Count(), Count()
            rels, atts, convs, pvs, lats = Count(), Count(), Count(), [0], []
            roped_n, scaled_n = [0], [0]
            free = {}

            def wait_bank(*banks):
                for b in banks:
                    if b in free:
                        pe.wait_ge(*free[b])

            def turn(bank, pos, src, part=P):
                return pe.transpose(T[bank][:, pos:pos + part], src, ident[0:part, 0:part])

            def columns(c, k, width, operand, start, stop, g):
                hi, lo = operand
                slot = chunk.now % RING
                for t in range(NT):
                    o = acc[g][t][:, 0:width]
                    l, m = hi[:, t * P:(t + 1) * P], lo[:, t * P:(t + 1) * P]
                    pe.matmul(o, l, w_hi[:, slot, k, 0:width], start=start, stop=False)
                    pe.matmul(o, l, w_lo[:, slot, k, 0:width], start=False, stop=False)
                    last = pe.matmul(o, m, w_hi[:, slot, k, 0:width], start=False, stop=stop)
                return last

            def stationary(kind, kt):
                if kind == "x":
                    return xT_hi[:, kt], xT_lo[:, kt]
                if kind in ("y", "ya"):
                    return y_hi[:, kt], y_lo[:, kt]
                if kind == "yb":
                    return y_hi[:, 8 + kt], y_lo[:, 8 + kt]
                if kind == "m":
                    return m_hl[:, kt // 4, 0, kt % 4], m_hl[:, kt // 4, 1, kt % 4]
                if kind == "f":
                    return f_hi[:, kt], f_lo[:, kt]
                if kind == "cq":
                    return cqT[:, 0, kt], cqT[:, 1, kt]
                return ckvT[:, 0, kt], ckvT[:, 1, kt]

            def stream(g, width, ks, kind, need=None, steps=None, table=True):
                if g is None or g >= 2:
                    pe.wait_ge(acc_taken[group.now % 2], 2 * group.turns(2))
                for c, kc in enumerate(ks):
                    if need and c in need:
                        pe.wait_ge(*need[c])
                    pe.wait_ge(w_split_lo, chunk.value(1))
                    for k in range(KC):
                        last = columns(c, k, width, stationary(kind, kc * KC + k),
                                       c == 0 and k == 0, c == len(ks) - 1 and k == KC - 1, group.now % 2)
                    last.then_inc(w_used, 1)
                    chunk.now += 1
                    if table:
                        run(chunk.now - 1)
                    if steps and c in steps:
                        steps[c]()
                group.now += 1

            def turn_ki():
                wait_bank(0)
                pe.wait_ge(acc_taken[0], 2)
                turn(0, 0, kdup[:, 0])
                turn(0, P, kdup[:, 1]).then_inc(copy_full, 1)
                copies.now += 1
                free[0] = (copy_done, copies.now)

            def four(bank, pick, done, n):
                for cc in range(2):
                    for t in range(NT):
                        last = turn(bank, cc * S + t * P, pick(cc, t))
                last.then_inc(done, 1)

            def turn_copy(name, g):
                if name in ("q1", "k1"):
                    scaled_n[0] += 1
                    pe.wait_ge(heads_scaled, scaled_n[0])
                elif name in ("qa", "ka", "qr"):
                    roped_n[0] += 1
                    pe.wait_ge(roped, roped_n[0])
                else:
                    pe.wait_ge(acc_taken[g % 2], 2 * (g // 2 + 1))
                for b in range(2):
                    wait_bank(b)
                    four(b, lambda cc, t: stage[:, g % 2, t, (2 * b + cc) * P:(2 * b + cc + 1) * P], copy_full, 1)
                    copies.now += 1
                    free[b] = (copy_done, copies.now)

            def on_rel(u):
                wait_bank(2, 3)
                pe.wait_ge(copy_done, 5)
                blk, h0, nh, nk = rel_unit(u)
                for k in range(nh):
                    h = h0 + k
                    r = IDX_DIM * (h % 2)
                    last = pe.matmul(T[2 + h % 2][:, (k // 2) * nk:(k // 2 + 1) * nk],
                                     qiT[r:r + IDX_DIM, h // 2, blk * P:(blk + 1) * P],
                                     kiT[r:r + IDX_DIM, 0:nk], start=True, stop=True)
                last.then_inc(rel_full, 1)
                rels.now += 1
                free[2] = free[3] = (rel_done, rels.now)

            def operands(which, pair, j):
                if which == "one":
                    return q1T[:, 2 * pair + j], k1T[:, 2 * pair + j], v1[:, :, (2 * pair + j) * HD:(2 * pair + j + 1) * HD]
                if which == "moba":
                    h = 2 * (pair % 2) + j
                    return qaT[:, h], kaT[:, h], va[:, :, h * HD:(h + 1) * HD]
                return qnT[:, 2 * pair + j], knT[:, pair % 2, j], vb[:, pair % 2, :, j * HD:(j + 1) * HD]

            def on_scores(which, pair):
                wait_bank(2, 3)
                pe.wait_ge(copy_done, copies.now)
                for blk in range(2):
                    nk = P * (blk + 1)
                    for j in range(2):
                        q, k, _ = operands(which, pair, j)
                        o = T[2 + blk][:, j * nk:(j + 1) * nk]
                        last = pe.matmul(o, q[:, blk * P:(blk + 1) * P], k[:, 0:nk], start=True, stop=which != "mla")
                        if which == "mla":
                            last = pe.matmul(o, qrT[:, pair, blk * P:(blk + 1) * P], krT[:, j, 0:nk],
                                             start=False, stop=True)
                last.then_inc(scores_full, 1)
                atts.now += 1
                free[2] = free[3] = (scores_masked, atts.now)

            def on_turn_p(which):
                wait_bank(0, 1)
                pe.wait_ge(p_ready, atts.now)
                for j in range(2):
                    turn(0, j * S, pbuf[:, j * P:(j + 1) * P])
                    last = turn(0, j * S + P, pbuf[:, S + j * S:S + j * S + P])
                last.then_inc(copy_full, 1)
                for j in range(2):
                    last = turn(1, j * P, pbuf[:, S + j * S + P:S + (j + 1) * S])
                last.then_inc(copy_full, 1)
                copies.now += 2
                free[0], free[1] = (copy_done, copies.now - 1), (copy_done, copies.now)
                pvs[0] = copies.now

            def on_pv(which, pair):
                wait_bank(2)
                pe.wait_ge(copy_done, pvs[0])
                for j in range(2):
                    v = operands(which, pair, j)[2]
                    pe.matmul(T[2][:, j * S:(j + 1) * S], v[:, 0], pT[:, j * S:(j + 1) * S], start=True, stop=False)
                    last = pe.matmul(T[2][:, j * S + P:(j + 1) * S], v[:, 1], pT[:, 2 * S + j * P:2 * S + (j + 1) * P],
                                     start=False, stop=True)
                last.then_inc(split_full, 1)
                splits.now += 1
                free[2] = (split_lo, splits.now)

            def on_pool_d(n, g):
                wait_bank(0, 1)
                pe.wait_ge(acc_taken[g % 2], 2 * (g // 2 + 1))
                for cc in range(4):
                    o, w = T[cc // 2][:, (cc % 2) * S:(cc % 2 + 1) * S], 2 * n + cc // 2
                    st = stage[:, g % 2, :, cc * P:(cc + 1) * P]
                    pe.matmul(o, st[:, 0], pool_m[:, w, 0:S], start=True, stop=False)
                    last = pe.matmul(o[:, P:S], st[:, 1], pool_m[:, w, S:KEYS], start=False, stop=True)
                    if cc % 2:
                        last.then_inc(copy_full, 1)
                        copies.now += 1
                        free[cc // 2] = (copy_done, copies.now)

            def on_pool_y(n):
                wait_bank(2, 3)
                pe.wait_ge(copy_done, copies.now)
                pe.wait_ge(pool_loaded, 16)
                for w in range(2):
                    for dc in range(2):
                        o = T[2 + w][:, dc * S:(dc + 1) * S]
                        for cc in range(2):
                            last = pe.matmul(o, pool_w[:, 2 * n + w, cc, dc * P:(dc + 1) * P], dT[:, 2 * w + cc],
                                             start=cc == 0, stop=cc == 1)
                    last.then_inc(split_full, 1)
                    splits.now += 1
                    free[2 + w] = (split_lo, splits.now)

            def on_turn_x(n, g):
                pe.wait_ge(acc_taken[g % 2], 2 * (g // 2 + 1))
                for b in range(2):
                    wait_bank(b)
                    four(b, lambda cc, t: x[:, t, n * CW + (2 * b + cc) * P:n * CW + (2 * b + cc + 1) * P], split_full, 1)
                    splits.now += 1
                    free[b] = (split_lo, splits.now)

            def on_turn_stage(g, banks, wait):
                pe.wait_ge(*wait)
                for b in banks:
                    wait_bank(b)
                    four(b, lambda cc, t: stage[:, g % 2, t, (2 * b + cc) * P:(2 * b + cc + 1) * P], split_full, 1)
                    splits.now += 1
                    free[b] = (split_lo, splits.now)

            def on_turn_lat(kind, g):
                on_turn_stage(g, range(2 if kind == "cq" else 1), (acc_taken[g % 2], 2 * (g // 2 + 1)))
                lats.append(splits.now)

            def on_turn_mix(g):
                mix_n[0] += 1
                on_turn_stage(0, range(2), (mixed, mix_n[0]))

            def on_turn_kr():
                wait_bank(0)
                roped_n[0] += 1
                pe.wait_ge(roped, roped_n[0])
                turn(0, 0, krd[:, 0])
                turn(0, P, krd[:, 1]).then_inc(copy_full, 1)
                copies.now += 1
                free[0] = (copy_done, copies.now)

            def on_turn_kn(k, g):
                wait_bank(0)
                pe.wait_ge(acc_taken[g % 2], 2 * (g // 2 + 1))
                four(0, lambda cc, t: stage[:, g % 2, t, 2 * cc * P:(2 * cc + 1) * P], copy_full, 1)
                copies.now += 1
                free[0] = (copy_done, copies.now)

            mix_n = [0]
            mine = {"turn_ki": turn_ki, "turn_copy": turn_copy, "rel": on_rel, "scores": on_scores,
                    "turn_p": on_turn_p, "pv": on_pv, "pool_d": on_pool_d, "pool_y": on_pool_y,
                    "turn_x": on_turn_x, "turn_lat": on_turn_lat, "turn_mix": on_turn_mix,
                    "turn_kr": on_turn_kr, "turn_kn": on_turn_kn}

            def run(n):
                for step_, *args in at.get(n, []):
                    if step_ in mine:
                        mine[step_](*args)

            pe.wait_ge(rows_loaded, 16 * 13)
            pe.wait_ge(const_loaded, 16 * 5)
            turn(0, 0, rows[0:G_ROWS, 0:P], G_ROWS)
            for k in range(4):
                last = turn(0, G_ROWS + k * CT, rows[0:CT, (k + 1) * P:(k + 2) * P], CT)
            last.then_inc(cols_turned, 1)
            free[0] = (cols_ready, 1)
            pe.wait_ge(x_loaded, 32)
            for m in range(KT // 2):
                b = (m + 1) % 4
                wait_bank(b)
                four(b, lambda cc, t: x[:, t, (2 * m + cc) * P:(2 * m + cc + 1) * P], split_full, 1)
                splits.now += 1
                free[b] = (split_lo, splits.now)

            def turned(par, banks, done):
                for b in banks:
                    four(b, lambda cc, t: stage[:, par, t, (2 * (b % 2) + cc) * P:(2 * (b % 2) + cc + 1) * P], done, 1)

            def taken_before(par):
                pe.wait_ge(acc_taken[par], 2 * group.turns(2, -1) + 2)

            def turn_conv(par, banks, first=False):
                taken_before(par)
                if first:
                    wait_bank(*banks)
                else:
                    pe.wait_ge(conv_done, convs.value())
                turned(par, banks, conv_full)
                convs.now += 2

            def turn_product(par):
                taken_before(par)
                pe.wait_ge(split_lo, splits.value())
                turned(0, (0, 1), split_full)
                splits.now += 2

            def feed_forward(layer, need):
                par = group.now % 2
                whole = list(range(KT // KC))

                def pair(j):
                    first = isinstance(j, int)
                    if layer == 1:
                        gate_steps = {} if first else {1: lambda: turn_conv(1 - par, (2, 3))}
                        value_steps = {1: lambda: turn_conv(par, (0, 1), first)}
                    else:
                        gate_steps, value_steps = {} if first else {1: lambda: turn_product(1 - par)}, {}
                    stream(None, CW, whole, "x", need if first else None, gate_steps, first)
                    stream(None, CW, whole, "x", None, value_steps, first)
                if layer == 1:
                    wait_bank(2, 3)
                counts = {"chunk": chunk, "group": group, "splits": splits, "convs": convs}
                per = {"chunk": 16, "group": 2, "splits": 0 if layer == 1 else 2,
                       "convs": 4 if layer == 1 else 0}
                with_loop(pe, counts, pair, per)
                return {1: lambda: turn_conv(1 - par, (2, 3)) if layer == 1 else turn_product(1 - par)}

            g, steps = 0, None
            while g < len(groups):
                name, col, width, ks, kind = groups[g]
                now, need = splits.now, {}
                if g == 0:
                    need = {c: (split_lo, c + 1) for c in range(8)}
                elif name == "w_out" and col == 0:
                    need = {0: (split_lo, 13), 5: (split_lo, 14), 6: (split_lo, 15), 7: (split_lo, 16)}
                elif g in (G_UP1, G_UP2, G_IN2) or name == "w_out_2" and col == 0:
                    need = {0: (split_lo, now), 6: (split_lo, now + 1), 7: (split_lo, now + 2)}
                elif name == "w_down" and col == 0:
                    need = {c: (f_ready, c // 2 + 1) for c in range(0, FT // KC, 2)}
                elif name == "w_down_2" and col == 0:
                    need = {c: (split_lo, now - 2 * (PAIRS - 1) + c + 1) for c in range(FT // KC)}
                elif name == "w_uq_2" and col == 0:
                    need = {0: (split_lo, lats[0])}
                elif name == "w_ukv_2" and col == 0:
                    need = {0: (split_lo, lats[1])}
                elif name == "w_branch_a_2" and col == 0:
                    need = {0: (split_lo, now)}
                if g in (G_UP1, G_UP2):
                    steps = feed_forward(1 if g == G_UP1 else 2, need)
                    g += 2 * PAIRS
                else:
                    stream(g, width, ks, kind, need, steps)
                    steps = None
                    g += 1
            for n in range(n_end, n_end + 8):
                run(n)

        @block.scalar
        def _(act):
            chunk, loads, group = Count(), [Count() for _ in range(RING)], Count()
            splits, copies, convs, hiddens, silus = Count(), Count(), Count(), Count(), Count()
            n_rstd, n_squared, n_att, n_rel, n_lat = [0], [0], [0], [0], [0]

            def split(name, width):
                slot = chunk.now % RING
                loads[slot].now += 2 if name == "w_uq_2" else 1
                act.wait_ge(w_loaded[slot], loads[slot].sixteens())
                if chunk.per or chunk.now >= RING:
                    act.wait_ge(w_used, chunk.value(1 - RING))
                act.activation(w_hi[:, slot, :, 0:width], w_raw[:, slot, :, 0:width], ACT.Copy).then_inc(w_split_hi, 1)
                chunk.now += 1

            def finished(g):
                act.wait_ge(w_used, first[g] + len(groups[g][3]))

            def taken(g):
                return acc_taken[g % 2], 2 * (g // 2 + 1)

            def on_evac(kind, g, *dest):
                finished(g)
                name, _, width, _, _ = groups[g]
                act.wait_ge(rstd_ready, n_rstd[0])
                if name in ("w_uq_2", "w_ukv_2"):
                    act.wait_ge(lat_rstd, 2)
                for t in range(NT):
                    scale = rstd[:, t:t + 1]
                    if name in ("w_uq_2", "w_ukv_2"):
                        k = 0 if name == "w_uq_2" else 1
                        scale = lrstd[:, k, t:t + 1]
                    src = acc[g % 2][t][:, 0:width]
                    if kind == "v":
                        o = v1[:, t, dest[1] * CW:(dest[1] + 1) * CW]
                    elif kind == "va":
                        o = va[:, t]
                    elif kind == "gate":
                        o = gate[:, dest[1], dest[0], t]
                    else:
                        o = stage[:, g % 2, t, 0:width]
                    if kind == "ukv":
                        act.activation(vb[:, dest[0] % 2, t].rearrange("p (h e) -> p h e", h=2),
                                       src.rearrange("p (h a e) -> p h a e", h=2, a=2)[:, :, 1], ACT.Copy, scale=scale)
                        o = o.rearrange("p (h a e) -> p h a e", h=2, a=2)[:, :, 0]
                        src = src.rearrange("p (h a e) -> p h a e", h=2, a=2)[:, :, 0]
                    act.activation(o, src, ACT.Copy, scale=scale).then_inc(acc_taken[g % 2], 1)

            def copied(out_, bank, width=CW, scale=1.0):
                copies.now += 1
                act.wait_ge(copy_full, copies.now)
                act.activation(out_, T[bank][:, 0:width], ACT.Copy, scale=scale).then_inc(copy_done, 1)

            def on_copy_ki():
                copied(kiT[:], 0, S)

            def on_copy2(name, half):
                act.wait_ge(cols_ready, 2)
                for b in range(2):
                    dest, k = {"qi": (qiT, 4), "q1": (q1T, 4), "k1": (k1T, 4), "qa": (qaT, 0), "ka": (kaT, 0),
                               "qn": (qnT, 4), "qr": (qrT, 0)}[name]
                    scale = {"k1": gqk[:], "qa": HD ** -0.5, "qn": (HD + ROPE_B) ** -0.5, "qr": (HD + ROPE_B) ** -0.5}.get(name, 1.0)
                    o = dest[:, k * half + 2 * b:k * half + 2 * b + 2].rearrange("p a b -> p (a b)")
                    copied(o, b, CW, scale)

            def on_relu(u):
                n_rel[0] += 1
                act.wait_ge(rel_full, n_rel[0])
                if n_rel[0] > 1:
                    act.wait_ge(isc_added, n_rel[0] - 1)
                act.activation(rel[:, 0:CW], T[2][:], ACT.Relu)
                act.activation(rel[:, CW:2 * CW], T[3][:], ACT.Relu).then_inc(rel_done, 1)

            def on_exp(which):
                n_att[0] += 1
                act.wait_ge(scores_masked, n_att[0])
                for k in range(4):
                    blk, j = k // 2, k % 2
                    nk = P * (blk + 1)
                    v = pbuf[:, blk * S + j * nk:blk * S + (j + 1) * nk]
                    last = act.activation(v, v, ACT.Exp, bias=negmax[:, k:k + 1], accum_out=psum_[:, k:k + 1])
                last.then_inc(exp_done, 1)

            def on_copy_p(which):
                copied(pT[:, 0:2 * S], 0)
                copied(pT[:, 2 * S:3 * S], 1, S)

            def on_copy_d(n):
                for b in range(2):
                    copied(dT[:, 2 * b:2 * b + 2].rearrange("p a b -> p (a b)"), b)

            def on_copy_kr():
                copies.now += 1
                act.wait_ge(copy_full, copies.now)
                act.wait_ge(kr_zeroed, 1)
                act.activation(krT[0:64, 0], T[0][0:64, 0:S], ACT.Copy)
                act.activation(krT[64:128, 1], T[0][64:128, 0:S], ACT.Copy).then_inc(copy_done, 1)

            def on_copy_kn(k):
                copied(knT[:, k % 2].rearrange("p a b -> p (a b)"), 0)

            def high(outs, bank, gain=None):
                splits.now += 1
                act.wait_ge(split_full, splits.now)
                n = len(outs)
                for k, o in enumerate(outs):
                    w = CW // n
                    scale = 1.0 if gain is None else cols[:, gain + k:gain + k + 1]
                    last = act.activation(o, T[bank][:, k * w:(k + 1) * w], ACT.Copy, scale=scale)
                last.then_inc(split_hi, 1)

            def on_split_y(which, pair):
                k = 2 * pair + (0 if which == "moba" else 8)
                high([y_hi[:, k:k + 2].rearrange("p a b -> p (a b)")], 2)

            def on_split_x(n, gain, b):
                k = 4 * n + 2 * b
                high([xT_hi[:, k], xT_hi[:, k + 1]], b, gain + k)

            def on_split_pool(n):
                for w in range(2):
                    k = 4 * n + 2 * w
                    high([y_hi[:, k], y_hi[:, k + 1]], 2 + w, G_POOL + k)

            def on_split_lat(kind):
                o, gain = (cqT, G_CQ) if kind == "cq" else (ckvT, G_CKV)
                for b in range(2 if kind == "cq" else 1):
                    high([o[:, 0, 2 * b], o[:, 0, 2 * b + 1]], b, gain + 2 * b)

            def on_split_mix(n):
                for b in range(2):
                    high([m_hl[:, n, 0, 2 * b:2 * b + 2].rearrange("p a b -> p (a b)")], b)

            def square(src, k, dest):
                if n_squared[0]:
                    act.wait_ge(squared, n_squared[0])
                act.activation(junk[:, k * CW:(k + 1) * CW][:, 0:src.shape[1]], src, ACT.Square, accum_out=dest).then_inc(squared, 1)
                n_squared[0] += 1

            def on_square(g, n):
                act.wait_ge(*taken(g))
                for t in range(NT):
                    square(x[:, t, n * CW:(n + 1) * CW], t, sumsq[:, t, n:n + 1])

            def on_lat_square(kind, g):
                act.wait_ge(*taken(g))
                k, w = (0, 512) if kind == "cq" else (1, 256)
                for t in range(NT):
                    square(stage[:, g % 2, t, 0:w], t, lsum[:, k, t:t + 1])

            def on_rstd():
                n_rstd[0] += 1

            def on_sigmoid(n):
                for k in range(2):
                    act.wait_ge(acc_taken[k], last_gate[k])
                v = gate[:, n].rearrange("p a b c -> p (a b c)")
                act.activation(v, v, ACT.Sigmoid).then_inc(gates_open, 1)

            mine = {"evac": on_evac, "copy_ki": on_copy_ki, "copy2": on_copy2, "relu": on_relu, "exp": on_exp,
                    "copy_p": on_copy_p, "copy_d": on_copy_d, "copy_kr": on_copy_kr, "copy_kn": on_copy_kn,
                    "split_y": on_split_y, "split_x": on_split_x, "split_pool": on_split_pool,
                    "split_lat": on_split_lat, "split_mix": on_split_mix, "square": on_square,
                    "lat_square": on_lat_square, "rstd": on_rstd, "sigmoid": on_sigmoid}

            def run(n):
                for step_, *args in at.get(n, []):
                    if step_ in mine:
                        mine[step_](*args)

            act.wait_ge(cols_turned, 1)
            act.activation(cols[:], T[0][:, 0:G_ROWS + 4 * CT], ACT.Copy).then_inc(cols_ready, 1)
            act.wait_ge(cols_ready, 1)
            act.wait_ge(x_loaded, 32)
            for m in range(KT // 2):
                high([xT_hi[:, 2 * m], xT_hi[:, 2 * m + 1]], (m + 1) % 4, G_ATTN1 + 2 * m)
                if m == 3:
                    for c in range(2):
                        split("w_in", groups[0][2])
            for n in range(4):
                for t in range(NT):
                    square(x[:, t, n * CW:(n + 1) * CW], t, sumsq[:, t, n:n + 1])
            n_rstd[0] = 1
            act.wait_ge(angles, 1)
            act.activation(sin[:], sin[:], ACT.Sin).then_inc(tables, 1)
            act.activation(cos[:], cos[:], ACT.Sin).then_inc(tables, 1)

            def evac_hidden(par):
                act.wait_ge(w_used, chunk.value(-LEAD - 1))
                act.wait_ge(rstd_ready, n_rstd[0])
                for t in range(NT):
                    act.activation(stage[:, par, t], acc[par][t][:], ACT.Copy, scale=rstd[:, t:t + 1]).then_inc(acc_taken[par], 1)

            def seed(bank, dest, j, base):
                convs.now += 1
                act.wait_ge(conv_full, convs.value())
                for cc in range(2):
                    k = CONV_COL + base + 2 * (bank % 2) + cc
                    last = act.activation(dest[:, 2 * (bank % 2) + cc], T[bank][:, cc * S:(cc + 1) * S], ACT.Identity,
                                          scale=cols[:, bass.ds(j * 4 + (k + 2 * CT), 1)],
                                          bias=cols[:, bass.ds(j * 4 + (k + 3 * CT), 1)])
                last.then_inc(conv_seeded, 1)

            def silu():
                act.wait_ge(conv_done, convs.value())
                act.activation(half_a[:], half_a[:], ACT.Silu).then_inc(silu_done, 1)

            def hidden_high(j):
                hiddens.now += 1
                act.wait_ge(hidden, hiddens.value())
                act.activation(f_hi[:, bass.ds(j * 4, 4)], half_b[:], ACT.Copy).then_inc(hidden_hi, 1)

            def gate_silu(par):
                act.wait_ge(w_used, chunk.value(-LEAD - 1))
                act.wait_ge(rstd_ready, n_rstd[0])
                for t in range(NT):
                    act.activation(half_a[:].rearrange("p (t a) b -> p t (a b)", t=NT)[:, t], acc[par][t][:], ACT.Silu,
                                   scale=rstd[:, t:t + 1]).then_inc(acc_taken[par], 1)

            def product_high(j):
                for b in range(2):
                    splits.now += 1
                    act.wait_ge(split_full, splits.value())
                    act.activation(f_hi[:, bass.ds(j * 4 + 2 * b, 2)].rearrange("p a b -> p (a b)"), T[b][:], ACT.Copy).then_inc(split_hi, 1)

            def feed_forward(layer, g0):
                par = g0 % 2

                def value_steps(j):
                    if layer == 1:
                        return {0: lambda: evac_hidden(1 - par), 2: lambda: seed(2, half_b, j, FT),
                                3: lambda: seed(3, half_b, j, FT), 5: lambda: hidden_high(j)}
                    return {2: lambda: product_high(j)}

                def pair(j):
                    first_ = isinstance(j, int)
                    steps = {} if first_ else value_steps(j - 1)
                    if layer == 1:
                        steps.update({8: lambda: evac_hidden(par), 10: lambda: seed(0, half_a, j, 0),
                                      11: lambda: seed(1, half_a, j, 0), 12: silu})
                    else:
                        steps.update({8: lambda: gate_silu(par)})
                    for c in range(2 * KT // KC):
                        split("w_up", CW)
                        if first_:
                            run(chunk.now - 1 - LEAD)
                        if c - LEAD in steps:
                            steps[c - LEAD]()
                counts = {"chunk": chunk, "splits": splits, "convs": convs, "hiddens": hiddens}
                counts.update({f"load{k}": loads[k] for k in range(RING)})
                per = {"chunk": 16, "splits": 0 if layer == 1 else 2, "convs": 4 if layer == 1 else 0,
                       "hiddens": 1 if layer == 1 else 0}
                per.update({f"load{k}": 16 // RING for k in range(RING)})
                with_loop(act, counts, pair, per)
                return value_steps(PAIRS - 1)

            last_gate = [max(2 * (g // 2 + 1) for g in gate_groups if g % 2 == k) for k in range(2)]
            g, steps = 0, {}
            while g < len(groups):
                if g in (G_UP1, G_UP2):
                    steps = feed_forward(1 if g == G_UP1 else 2, g)
                    g += 2 * PAIRS
                    continue
                name, _, width, ks, _ = groups[g]
                for c in range(len(ks)):
                    if chunk.now < first[g] + c + 1:
                        split(name, width)
                    if chunk.now - 1 - LEAD >= 0:
                        run(first[g] + c - LEAD)
                    if c - LEAD in steps:
                        steps[c - LEAD]()
                steps = {}
                g += 1
            for n in range(n_end - LEAD, n_end + 8):
                run(n)

        @block.vector
        def _(dve):
            chunk = Count()
            step_n, splits, convs, seeds, hiddens, silus = Count(), Count(), Count(), Count(), Count(), Count()
            takens = [Count(), Count()]
            n_rstd, n_squared, n_att, n_rel, n_lat, n_heads, n_scaled = [0], [0], [0], [0], [0], [0], [0]

            def link(ins):
                ins.then_inc(dve_step, 1)
                step_n.now += 1

            def linked():
                dve.wait_ge(dve_step, step_n.value())

            def split(width):
                slot = chunk.now % RING
                chunk.now += 1
                dve.wait_ge(w_split_hi, chunk.value())
                dve.tensor_tensor(w_lo[:, slot, :, 0:width], w_raw[:, slot, :, 0:width],
                                  w_hi[:, slot, :, 0:width].bitcast(F32), ALU.subtract).then_inc(w_split_lo, 1)

            def finished(g):
                dve.wait_ge(w_used, first[g] + len(groups[g][3]))

            def on_evac_kw(g):
                finished(g)
                dve.wait_ge(rstd_ready, 1)
                for t in range(NT):
                    r = rstd[:, t:t + 1]
                    dve.tensor_scalar(widx[:, t], acc[0][t][:, 64:80], r, 2.0 ** -5, ALU.mult, ALU.mult)
                    dve.tensor_scalar(kdup[:, t, 0:64], acc[0][t][:, 0:64], r, None, ALU.mult)
                    dve.tensor_scalar(kdup[:, t, 64:128], acc[0][t][:, 0:64], r, None, ALU.mult).then_inc(acc_taken[0], 1)

            def on_headsq(name, g):
                dve.wait_ge(acc_taken[g % 2], 2 * (g // 2 + 1))
                for t in range(NT):
                    st = stage[:, g % 2, t]
                    if step_n.now:
                        linked()
                    link(dve.tensor_tensor(hsq[:], st, st, ALU.mult))
                    linked()
                    link(dve.tensor_reduce(hsum[:, t], hsq[:].rearrange("p (h e) -> p h e", h=4), AX.X, ALU.add))
                linked()
                mul, add = (1.0, HD * EPS) if name == "q1" else (1.0 / HD, EPS)
                dve.tensor_scalar(hmean[:], hsum[:], mul, add, ALU.mult, ALU.add).then_inc(heads_mean, 1)

            def on_headscale(name, g):
                n_heads[0] += 1
                dve.wait_ge(heads_rstd, n_heads[0])
                for t in range(NT):
                    st = stage[:, g % 2, t].rearrange("p (h e) -> p h e", h=4)
                    last = dve.tensor_tensor(st, st, hrstd[:, t].unsqueeze(2).to_broadcast([P, 4, HD]), ALU.mult)
                last.then_inc(heads_scaled, 1)

            def on_isc(u):
                n_rel[0] += 1
                dve.wait_ge(rel_done, n_rel[0])
                blk, h0, nh, nk = rel_unit(u)
                o = isc[:, blk * P:blk * P + nk]
                for k in range(nh):
                    r = rel[:, (k % 2) * CW + (k // 2) * nk:(k % 2) * CW + (k // 2 + 1) * nk]
                    w = widx[:, blk, h0 + k:h0 + k + 1]
                    if h0 + k == 0:
                        last = dve.tensor_scalar(o, r, w, None, ALU.mult)
                    else:
                        linked()
                        last = dve.scalar_tensor_tensor(o, r, w, o, ALU.mult, ALU.add)
                    link(last)
                linked()
                dve.sem_inc(isc_added, 1)

            def on_topk(r):
                if r == 0:
                    link(dve.tensor_tensor(isc[:], isc[:], causal[:], ALU.min))
                linked()
                src = isc[:] if r == 0 else picked[:, (r - 1) % 2]
                spans = ((0, P), (P, KEYS))
                for k, (lo_, hi_) in enumerate(spans):
                    link(dve.max(top8[:, k], src[:, lo_:hi_]))
                linked()
                for k, (lo_, hi_) in enumerate(spans):
                    link(dve.match_replace(picked[:, r % 2, lo_:hi_], top8[:, k], src[:, lo_:hi_], FMIN))

            def on_select():
                linked()
                link(dve.tensor_tensor(sel[:], picked[:, (TOPK // 8 - 1) % 2], isc[:], ALU.is_lt))
                linked()
                link(dve.tensor_scalar(sel[:], sel[:], 0.5, BIG, ALU.subtract, ALU.mult))

            def on_mask(which):
                n_att[0] += 1
                dve.wait_ge(scores_full, n_att[0])
                m = sel if which == "one" else causal
                if which == "one":
                    linked()
                for blk in range(2):
                    nk = P * (blk + 1)
                    v = pbuf[:, blk * S:blk * S + 2 * nk].rearrange("p (j n) -> p j n", j=2)
                    link(dve.tensor_tensor(v, T[2 + blk][:, 0:2 * nk].rearrange("p (j n) -> p j n", j=2),
                                           m[:, blk * P:blk * P + nk].unsqueeze(1).to_broadcast([P, 2, nk]), ALU.min))
                linked()
                for blk in range(2):
                    nk = P * (blk + 1)
                    v = pbuf[:, blk * S:blk * S + 2 * nk].rearrange("p (j n) -> p j n", j=2)
                    last = dve.tensor_reduce(negmax[:, 2 * blk:2 * blk + 2], v, AX.X, ALU.max, negate=True)
                last.then_inc(scores_masked, 1)

            def on_norm(which):
                dve.wait_ge(exp_done, n_att[0])
                link(dve.reciprocal(pinv[:], psum_[:]))
                linked()
                for blk in range(2):
                    nk = P * (blk + 1)
                    v = pbuf[:, blk * S:blk * S + 2 * nk].rearrange("p (j n) -> p j n", j=2)
                    last = dve.tensor_tensor(v, v, pinv[:, 2 * blk:2 * blk + 2].unsqueeze(2).to_broadcast([P, 2, nk]), ALU.mult)
                last.then_inc(p_ready, 1)

            def low(outs, his, bank, gain=None):
                splits.now += 1
                dve.wait_ge(split_hi, splits.now)
                n = len(outs)
                for k, (o, h) in enumerate(zip(outs, his)):
                    w = CW // n
                    b = T[bank][:, k * w:(k + 1) * w]
                    if gain is None:
                        last = dve.tensor_tensor(o, b, h.bitcast(F32), ALU.subtract)
                    else:
                        last = dve.scalar_tensor_tensor(o, b, cols[:, gain + k:gain + k + 1], h.bitcast(F32),
                                                        ALU.mult, ALU.subtract)
                last.then_inc(split_lo, 1)

            def on_split_y(which, pair):
                k = 2 * pair + (0 if which == "moba" else 8)
                low([y_lo[:, k:k + 2].rearrange("p a b -> p (a b)")], [y_hi[:, k:k + 2].rearrange("p a b -> p (a b)")], 2)

            def on_split_x(n, gain, b):
                k = 4 * n + 2 * b
                low([xT_lo[:, k], xT_lo[:, k + 1]], [xT_hi[:, k], xT_hi[:, k + 1]], b, gain + k)

            def on_split_pool(n):
                for w in range(2):
                    k = 4 * n + 2 * w
                    low([y_lo[:, k], y_lo[:, k + 1]], [y_hi[:, k], y_hi[:, k + 1]], 2 + w, G_POOL + k)

            def on_split_lat(kind):
                o, gain = (cqT, G_CQ) if kind == "cq" else (ckvT, G_CKV)
                for b in range(2 if kind == "cq" else 1):
                    low([o[:, 1, 2 * b], o[:, 1, 2 * b + 1]], [o[:, 0, 2 * b], o[:, 0, 2 * b + 1]], b, gain + 2 * b)

            def on_split_mix(n):
                for b in range(2):
                    v = m_hl[:, n, :, 2 * b:2 * b + 2].rearrange("p s a b -> p s (a b)")
                    low([v[:, 1]], [v[:, 0]], b)

            def on_res(g, n):
                finished(g)
                for t in range(NT):
                    v = x[:, t, n * CW:(n + 1) * CW]
                    dve.tensor_tensor(v, acc[g % 2][t][:], v, ALU.add).then_inc(acc_taken[g % 2], 1)

            def mean(sums):
                dve.wait_ge(squared, sums)
                link(dve.tensor_reduce(meansq[:], sumsq[:], AX.X, ALU.add))
                linked()
                dve.tensor_scalar(meansq[:], meansq[:], 1.0 / D, EPS, ALU.mult, ALU.add).then_inc(mean_ready, 1)

            def on_rstd():
                n_squared[0] += 8
                mean(n_squared[0])

            def on_lat_rstd(kind):
                n_squared[0] += 2
                dve.wait_ge(squared, n_squared[0])
                k = ("cq", "ckv").index(kind)
                dve.tensor_scalar(lmean[:, k], lsum[:, k], 1.0 / (512, 256)[k], EPS, ALU.mult, ALU.add).then_inc(lat_mean, 1)

            def on_turn_kr():
                dve.memset(krT[:], 0.0).then_inc(kr_zeroed, 1)

            def on_mix_a(n, g):
                finished(g)
                dve.wait_ge(gates_open, n + 1)
                for t in range(NT):
                    v = gate[:, n, 0, t]
                    last = dve.tensor_tensor(v, acc[g % 2][t][:], v, ALU.mult)
                    last.then_inc(acc_taken[g % 2], 1)

            def on_mix_b(n, g):
                finished(g)
                for t in range(NT):
                    v = gate[:, n, 1, t]
                    dve.tensor_tensor(v, acc[g % 2][t][:], v, ALU.mult).then_inc(acc_taken[g % 2], 1)
                dve.wait_ge(acc_taken[g % 2], 2 * (g // 2 + 1))
                for t in range(NT):
                    last = dve.tensor_tensor(stage[:, 0, t], gate[:, n, 0, t], gate[:, n, 1, t], ALU.add)
                last.then_inc(mixed, 1)

            mine = {"evac_kw": on_evac_kw, "headsq": on_headsq, "headscale": on_headscale, "isc": on_isc, "topk": on_topk,
                    "select": on_select, "mask": on_mask, "norm": on_norm, "split_y": on_split_y, "split_x": on_split_x,
                    "split_pool": on_split_pool, "split_lat": on_split_lat, "split_mix": on_split_mix, "res": on_res,
                    "rstd": on_rstd, "lat_rstd": on_lat_rstd, "mix_a": on_mix_a, "turn_kr": on_turn_kr, "mix_b": on_mix_b}

            def run(n):
                for step_, *args in at.get(n, []):
                    if step_ in mine:
                        mine[step_](*args)

            dve.memset(minus_half[:], -0.5).then_inc(consts_set, 1)
            dve.wait_ge(cols_ready, 1)
            for m in range(KT // 2):
                low([xT_lo[:, 2 * m], xT_lo[:, 2 * m + 1]], [xT_hi[:, 2 * m], xT_hi[:, 2 * m + 1]], (m + 1) % 4, G_ATTN1 + 2 * m)
                if m == 3:
                    for c in range(2):
                        split(groups[0][2])
            dve.tensor_tensor(gqk[:], cols[:, G_Q:G_Q + 1], cols[:, G_K:G_K + 1], ALU.mult).then_inc(cols_ready, 1)
            n_squared[0] = 8
            mean(8)

            ang, turns_, r_ = (rel[:, k * 128:k * 128 + 96].rearrange("p (t f) -> p t f", t=NT) for k in range(3))
            dve.wait_ge(const_loaded, 16 * 5)
            link(dve.tensor_copy(pos_f[:], pos_i[:])); linked()
            for t in range(NT):
                link(dve.tensor_scalar(ang[:, t], cos[:, 0], pos_f[:, t:t + 1], None, ALU.mult))
            linked()
            link(dve.tensor_scalar(turns_, ang, 1.0 / (2 * math.pi), ROUND, ALU.mult, ALU.add)); linked()
            link(dve.tensor_scalar(turns_, turns_, ROUND, None, ALU.subtract)); linked()
            src = ang
            for c in TWO_PI:
                link(dve.scalar_tensor_tensor(r_, turns_, -c, src, ALU.mult, ALU.add)); linked()
                src = r_
            link(dve.tensor_scalar(sin[:], r_, -math.pi + 1e-6, math.pi - 1e-6, ALU.max, ALU.min)); linked()
            link(dve.tensor_scalar(cos[:], sin[:], -1.0, None, ALU.mult)); linked()
            link(dve.tensor_tensor(cos[:], cos[:], sin[:], ALU.min)); linked()
            dve.tensor_scalar(cos[:], cos[:], math.pi / 2, None, ALU.add).then_inc(angles, 1)

            def convolve(bank, dest, j, base):
                seeds.now += 1
                dve.wait_ge(conv_seeded, seeds.value())
                for tap, back in ((1, 1), (0, 2)):
                    for cc in range(2):
                        k = CONV_COL + base + 2 * (bank % 2) + cc + tap * CT
                        o = dest[:, 2 * (bank % 2) + cc, back:S]
                        last = dve.scalar_tensor_tensor(o, T[bank][:, cc * S:(cc + 1) * S - back],
                                                        cols[:, bass.ds(j * 4 + k, 1)], o, ALU.mult, ALU.add)
                        if tap:
                            link(last)
                    if tap:
                        linked()
                last.then_inc(conv_done, 1)
                convs.now += 1

            def multiply():
                silus.now += 1
                dve.wait_ge(silu_done, silus.value())
                dve.wait_ge(conv_done, convs.value())
                dve.tensor_tensor(half_b[:], half_a[:], half_b[:], ALU.mult).then_inc(hidden, 1)

            def hidden_low(j):
                hiddens.now += 1
                dve.wait_ge(hidden_hi, hiddens.value())
                v = bass.ds(j * 4, 4)
                dve.tensor_tensor(f_lo[:, v], half_b[:], f_hi[:, v].bitcast(F32), ALU.subtract).then_inc(f_ready, 1)

            def product(par):
                dve.wait_ge(w_used, chunk.value(-LEAD - 1))
                for t in range(NT):
                    sg = half_a[:].rearrange("p (t a) b -> p t (a b)", t=NT)[:, t]
                    last = dve.scalar_tensor_tensor(stage[:, 0, t], acc[par][t][:], rstd[:, t:t + 1], sg, ALU.mult, ALU.mult)
                    if t == 0:
                        last.then_inc(acc_taken[par], 1)
                last.then_inc(acc_taken[par], 1)
                takens[par].now += 2

            def product_low(j):
                for b in range(2):
                    splits.now += 1
                    dve.wait_ge(split_hi, splits.value())
                    v = bass.ds(j * 4 + 2 * b, 2)
                    dve.tensor_tensor(f_lo[:, v].rearrange("p a b -> p (a b)"), T[b][:],
                                      f_hi[:, v].rearrange("p a b -> p (a b)").bitcast(F32), ALU.subtract).then_inc(split_lo, 1)

            def feed_forward(layer, g0):
                par = g0 % 2

                def value_steps(j):
                    if layer == 1:
                        return {2: lambda: convolve(2, half_b, j, FT), 3: lambda: convolve(3, half_b, j, FT),
                                4: multiply, 6: lambda: hidden_low(j)}
                    return {0: lambda: product(1 - par), 2: lambda: product_low(j)}

                def pair(j):
                    first_ = isinstance(j, int)
                    steps = {} if first_ else value_steps(j - 1)
                    if layer == 1:
                        steps.update({10: lambda: convolve(0, half_a, j, 0), 11: lambda: convolve(1, half_a, j, 0)})
                    for c in range(2 * KT // KC):
                        split(CW)
                        if first_:
                            run(chunk.now - 1 - LEAD)
                        if c - LEAD in steps:
                            steps[c - LEAD]()
                counts = {"chunk": chunk, "step": step_n, "splits": splits, "convs": convs, "seeds": seeds,
                          "hiddens": hiddens, "silus": silus}
                one = layer == 1
                per = {"chunk": 16, "step": 8 if one else 0, "splits": 0 if one else 2, "convs": 4 if one else 0,
                       "seeds": 4 if one else 0, "hiddens": 1 if one else 0, "silus": 1 if one else 0}
                with_loop(dve, counts, pair, per)
                return value_steps(PAIRS - 1)

            g, steps = 0, {}
            while g < len(groups):
                if g in (G_UP1, G_UP2):
                    steps = feed_forward(1 if g == G_UP1 else 2, g)
                    g += 2 * PAIRS
                    continue
                name, _, width, ks, _ = groups[g]
                for c in range(len(ks)):
                    if chunk.now < first[g] + c + 1:
                        split(width)
                    if chunk.now - 1 - LEAD >= 0:
                        run(first[g] + c - LEAD)
                    if c - LEAD in steps:
                        steps[c - LEAD]()
                steps = {}
                g += 1
            for n in range(n_end - LEAD, n_end + 8):
                run(n)
            dve.wait_ge(rstd_ready, 5)
            dve.wait_ge(fgain_loaded, 16)
            for t in range(NT):
                for h in range(2):
                    v = x[:, t, h * 1024:(h + 1) * 1024]
                    dve.scalar_tensor_tensor(v, v, rstd[:, t:t + 1], fgain[:, h * 1024:(h + 1) * 1024],
                                             ALU.mult, ALU.mult).then_inc(normalised, 1)


_FIRST = ["x", "attn_norm_g", "w_in", "pool_w", "pool_scale", "q_norm_g", "k_norm_g", "w_out", "ffn_norm_g", "w_up",
          "conv_w", "conv_b", "w_down", "positions_2", "final_norm_2"]
_LAYER = ["attn_norm_2", "w_in_2", "q_norm_2", "w_uq_2", "kv_norm_2", "w_ukv_2", "w_branch_a_2", "w_branch_b_2",
          "w_out_2", "ffn_norm_2", "w_gate_2", "w_up_2", "w_down_2"]


def shape_constants():
    t = np.arange(S)
    causal = np.where(t[None, :] <= t[:, None], np.float32(BIG), np.float32(FMIN)).astype(np.float32)
    pool = np.zeros((P, 4, KEYS), np.float32)
    for w, window in enumerate(WINDOWS):
        inside = (t[:, None] <= t[None, :]) & (t[:, None] > t[None, :] - window)
        m = inside / np.minimum(t + 1, window)[None, :] - np.eye(S)
        pool[:, w, 0:S], pool[:, w, S:] = m[0:P], m[P:, P:]
    freq = np.concatenate([ROPE_THETA ** (-np.arange(0, d, 2) / d) for d in (ROPE_A, ROPE_B)])
    return {"c_ident": np.eye(P, dtype=np.float32),
            "c_causal": np.ascontiguousarray(np.concatenate([causal[0:P, 0:P], causal[P:, :]], axis=1)),
            "c_pool": pool, "c_freq": np.ascontiguousarray(np.broadcast_to(freq.astype(np.float32), (P, 48)))}


def kernel(**inputs):
    import concourse.bacc as bacc
    from concourse.bass_utils import run_bass_kernel_spmd

    nc = bacc.Bacc("TRN2", target_bir_lowering=False, num_devices=1)
    arrays, views = {}, {}
    for name, value in [(n, inputs[n]) for n in _FIRST + _LAYER] + list(shape_constants().items()):
        value = np.ascontiguousarray(value)
        arrays[f"in_{name}"] = value
        view = nc.dram_tensor(f"in_{name}", value.shape, mybir.dt.from_np(value.dtype), kind="ExternalInput").ap()
        views[name] = view[0] if name in _LAYER else view
    out = nc.dram_tensor("out_0", (1, S, D), F32, kind="ExternalOutput").ap()
    two_layer_kernel(nc, views, out)
    result = run_bass_kernel_spmd(nc, [arrays], core_ids=[0])
    return result.results[0]["out_0"]
```

```python
import concourse.bass as bass
from concourse import mybir
from contextlib import ExitStack
import math
import numpy as np

F32 = mybir.dt.float32
F32R = mybir.dt.float32r
I32 = mybir.dt.int32
ALU = mybir.AluOpType
ACT = mybir.ActivationFunctionType
AX = mybir.AxisListType

P = 128
S = 256
NT = S // P
D = 2048
KT = D // P
CW = 512
KC = 2
KC_KW = 8
RING = 4
LEAD = 3
DFF = 5632
FT = DFF // P
PAIRS = DFF // CW
HD = 128
NH = 8
TOPK = 64
IDX_HEADS, IDX_DIM = 16, 64
KW = IDX_DIM + IDX_HEADS
WINDOWS = (2, 4, 8, 16)
ROPE_A, ROPE_B = 32, 64
EPS = 1e-6
FMIN = -3.4028234663852886e38
ROPE_THETA = 500000.0
ROUND = 1.5 * 2.0 ** 23
TWO_PI = (6.28125, 1.93500518798828125e-3, 3.019915981956753e-07)
BIG = 3.3e38
KEYS = P + S

G_ATTN1, G_FFN1, G_ATTN2, G_FFN2, G_POOL, G_CQ, G_CKV, G_Q, G_K = 0, 16, 32, 48, 64, 72, 76, 78, 79
G_ROWS = 80
CONV_COL = G_ROWS
CT = 2 * DFF // P


def rel_unit(u):
    return (0, 8 * u, 8, P) if u < 2 else (1, 4 * (u - 2), 4, S)


def plan():
    groups, first, at = [], [], {}

    def group(*g):
        first.append(first[-1] + len(groups[-1][3]) if groups else 0)
        groups.append(g)
        return first[-1] + len(g[3])

    def put(n, *step):
        at.setdefault(n, []).append(step)

    whole = list(range(KT // KC))

    def copy_out(n, kind, *dest):
        put(n, "evac", kind, len(groups) - 1, *dest)
        if kind == "stage" and dest[0] in ("q1", "k1"):
            put(n + 1, "headsq", dest[0], len(groups) - 1)
            put(n + 3, "headscale", dest[0], len(groups) - 1)
            put(n + 4, "turn_copy", dest[0], len(groups) - 1)
            put(n + 5, "copy2", *dest)
        elif kind == "stage" and dest[0] in ("qa", "ka"):
            put(n + 1, "rope", "a", len(groups) - 1)
            put(n + 4, "turn_copy", dest[0], len(groups) - 1)
            put(n + 5, "copy2", *dest)
        elif kind == "stage" and dest[0] == "qr":
            put(n + 1, "rope", "b", len(groups) - 1)
            put(n + 4, "turn_copy", dest[0], len(groups) - 1)
            put(n + 5, "copy2", *dest)
        elif kind == "stage":
            put(n + 1, "turn_copy", dest[0], len(groups) - 1)
            put(n + 2, "copy2", *dest)

    def attend(a, which, pair):
        put(a, "scores", which, pair)
        put(a + 1, "mask", which)
        put(a + 2, "exp", which)
        put(a + 3, "norm", which)
        put(a + 4, "turn_p", which)
        put(a + 5, "copy_p", which)
        put(a + 6, "pv", which, pair)
        put(a + 7, "split_y", which, pair)

    def residual(n, g, b, gain):
        put(b, "res", g, n)
        put(b + 1, "square", g, n)
        if gain is not None:
            put(b + 1, "turn_x", n, g)
            put(b + 2, "split_x", n, gain, 0)
            put(b + 3, "split_x", n, gain, 1)
        elif n < 3:
            put(b + 3, "times_gain", n)
        if n == 3:
            put(b + (3 if gain is not None else 1), "rstd")

    for n in range(4):
        put(n, "square0", n)
    put(4, "rstd0")
    put(5, "turn_taps"); put(6, "copy_taps")
    for n in range(2):
        b = group("w_in", 4096 + CW * n, CW, whole, "x")
        copy_out(b, "stage", "qi", n)
        if n == 0:
            b = group("w_in", 5120, KW, list(range(KT // KC_KW)), "kw")
            put(b, "copy_kw", len(groups) - 1); put(b + 1, "turn_kw", len(groups) - 1); put(b + 1, "evac_kw")
            put(b + 3, "turn_ki"); put(b + 4, "copy_ki")
    for u in range(6):
        put(b + 3 + 2 * u, "rel", u); put(b + 4 + 2 * u, "relu", u); put(b + 4 + 2 * u, "isc", u)
    for half in range(2):
        for name, col in (("q1", 1024), ("k1", 2048), ("v1", 3072)):
            b = group("w_in", col + CW * half, CW, whole, "x")
            copy_out(b, "v" if name == "v1" else "stage", name, half)
            if name == "q1" and half == 0:
                for r, n in enumerate((7, 8, 10, 12, 13, 14, 15, 16)):
                    put(b + n, "topk", r)
                put(b + 17, "select")
            if name == "v1":
                attend(b + 2 - 4 * half, "one", 2 * half); attend(b + 10 - 4 * half, "one", 2 * half + 1)
    for n in range(2):
        b = group("w_in", CW * n, CW, whole, "x")
        put(b, "evac", "stage", len(groups) - 1)
        put(b + 1, "pool_d", n, len(groups) - 1); put(b + 2, "copy_d", n)
        put(b + 3, "pool_y", n); put(b + 4, "split_pool", n)
    for n in range(4):
        b = group("w_out", CW * n, CW, [0, 1, 4, 5, 6, 7, 2, 3] if n == 0 else whole, "y")
        residual(n, len(groups) - 1, b, G_FFN1)
    up1 = b
    for j in range(PAIRS):
        group("w_up", CW * j, CW, whole, "x")
        b = group("w_up", DFF + CW * j, CW, whole, "x")
    put(b + 30, "angles")
    for n in range(4):
        b = group("w_down", CW * n, CW, list(range(FT // KC)), "f")
        residual(n, len(groups) - 1, b, G_ATTN2)
    b = group("w_in_2", 3072, 512, whole, "x")
    put(b, "evac", "stage", len(groups) - 1); put(b + 1, "lat_square", "cq", len(groups) - 1)
    put(b + 1, "turn_lat", "cq", len(groups) - 1)
    put(b + 2, "split_lat", "cq"); put(b + 2, "lat_rstd", "cq")
    b = group("w_in_2", 3584, 320, whole, "x")
    put(b, "evac", "ckv", len(groups) - 1); put(b + 1, "lat_square", "ckv", len(groups) - 1)
    put(b + 1, "turn_lat", "ckv", len(groups) - 1)
    put(b + 2, "split_lat", "ckv"); put(b + 2, "lat_rstd", "ckv"); put(b + 1, "rope", "kr", len(groups) - 1)
    put(b + 4, "turn_kr"); put(b + 5, "copy_kr")
    for name, col in (("qa", 0), ("ka", 1024), ("va", 2048)):
        b = group("w_in_2", col, CW, whole, "x")
        copy_out(b, "va" if name == "va" else "stage", name, 0)
    attend(b + 7, "moba", 0); attend(b + 15, "moba", 1)
    for n in range(3):
        b = group("w_uq_2", n, CW, [0, 1], "cq")
        copy_out(b, "stage", "qr" if n == 2 else "qn", n)
    for name, col in (("qa", 0), ("ka", 1024), ("va", 2048)):
        b = group("w_in_2", col + CW, CW, whole, "x")
        copy_out(b, "va" if name == "va" else "stage", name, 1)
    gates = [(0, 0), (1, 0), (0, 1), (1, 1), (0, 2), (1, 2), (0, 3), (1, 3)]
    for k, (ab, n) in enumerate(gates):
        if k < 4:
            b = group("w_ukv_2", CW * k, CW, [0], "ckv")
            put(b, "evac", "ukv", len(groups) - 1, k); put(b + 1, "turn_kn", k, len(groups) - 1)
            put(b + 2, "copy_kn", k)
            attend(b + 3, "mla", k)
        elif k < 6:
            attend(b + 3, "moba", k - 2)
        b = group("w_in_2", 3904 + ab * D + CW * n, CW, whole, "x")
        put(b, "evac", "gate", len(groups) - 1, ab, n)
    for n in range(4):
        b = group("w_branch_a_2", CW * n, CW, [0, 1, 2, 3], "ya")
        put(b, "sigmoid", n); put(b, "mix_a", n, len(groups) - 1)
        b = group("w_branch_b_2", CW * n, CW, [0, 1, 2, 3], "yb")
        put(b, "mix_b", n, len(groups) - 1); put(b + 1, "turn_mix", len(groups) - 1); put(b + 2, "split_mix", n)
    for n in range(4):
        b = group("w_out_2", CW * n, CW, whole, "m")
        residual(n, len(groups) - 1, b, G_FFN2)
    up2 = b
    for j in range(PAIRS):
        group("w_gate_2", CW * j, CW, whole, "x")
        b = group("w_up_2", CW * j, CW, whole, "x")
    for n in range(4):
        b = group("w_down_2", CW * n, CW, list(range(FT // KC)), "f")
        residual(n, len(groups) - 1, b, None)
    return groups, first, at, up1, up2, b


class Count:

    def __init__(self):
        self.now, self.i, self.per = 0, None, 0

    def value(self, more=0):
        return self.now + more + (self.i * self.per if self.per else 0)

    def sixteens(self):
        return 16 * self.now + (self.i * (16 * self.per) if self.per else 0)

    def turns(self, ring, more=0):
        assert self.per % ring == 0
        return (self.now + more) // ring + (self.i * (self.per // ring) if self.per else 0)


def two_layer_kernel(nc, a, out):
    groups, first, at, up1, up2, n_end = plan()
    G_UP1 = first.index(up1)
    G_UP2 = first.index(up2)
    G_IN2 = [g[0] for g in groups].index("w_in_2")
    gate_groups = [g for g, v in enumerate(groups) if v[0] == "w_in_2" and v[1] >= 3904]
    ctx = ExitStack()
    with ctx:
        def sb(name, shape, dt=F32, c=ctx):
            return c.enter_context(nc.sbuf_tensor(name, shape, dt))

        def sem(name):
            return ctx.enter_context(nc.semaphore(name))

        x = sb("x_res", [P, NT, D])
        xT_hi, xT_lo = sb("xT_hi", [P, KT, S], F32R), sb("xT_lo", [P, KT, S], F32R)
        w_raw = sb("w_raw", [P, RING, KC, CW])
        w_hi, w_lo = sb("w_hi", [P, RING, KC, CW], F32R), sb("w_lo", [P, RING, KC, CW], F32R)
        stage = sb("stage", [P, 2, NT, CW])
        halves = sb("halves", [P, 2, 4, S])
        half_a, half_b = halves[:, 0], halves[:, 1]
        ident = sb("ident", [P, P])
        causal = sb("causal", [P, KEYS])
        cols = sb("cols", [P, G_ROWS + 4 * CT])
        gqk = sb("gqk", [P, 1])
        cos, sin = sb("cos", [P, NT, 48]), sb("sin", [P, NT, 48])
        sumsq, meansq, rstd = sb("sumsq", [P, NT, 4]), sb("meansq", [P, NT]), sb("rstd", [P, NT])
        pos_i, pos_f = sb("pos_i", [P, NT], I32), sb("pos_f", [P, NT])
        minus_half = sb("minus_half", [P, 8])
        hsum, hmean, hrstd = sb("hsum", [P, NT, 4]), sb("hmean", [P, NT, 4]), sb("hrstd", [P, NT, 4])
        lsum, lmean = sb("lsum", [P, 2, NT]), sb("lmean", [P, 2, NT])
        lrstd = sb("lrstd", [P, 2, NT])
        negmax, psum_, pinv = sb("negmax", [P, 4]), sb("p_sum", [P, 4]), sb("p_inv", [P, 4])
        with ExitStack() as r:
            y_hi, y_lo = sb("y_hi", [P, KT, S], F32R, r), sb("y_lo", [P, KT, S], F32R, r)
            with ExitStack() as q:
                q1T, k1T = sb("q1T", [P, NH, S], F32, q), sb("k1T", [P, NH, S], F32, q)
                v1 = sb("v1", [P, NT, NH * HD], F32, q)
                with ExitStack() as s:
                    qiT = sb("qiT", [P, IDX_HEADS // 2, S], F32, s)
                pool_w = sb("pool_w", [P, 4, 2, S], F32, q)
                kiT = sb("kiT", [P, S], F32, q)
                kdup = sb("kdup", [P, NT, P], F32, q)
                widx = sb("widx", [P, NT, IDX_HEADS], F32, q)
                isc = sb("isc", [P, KEYS], F32, q)
                picked = sb("picked", [P, 2, KEYS], F32, q)
                top8 = sb("top8", [P, 2, 8], F32, q)
                sel = sb("sel", [P, KEYS], F32, q)
                hsq = sb("hsq", [P, CW], F32, q)
                pool_m = sb("pool_m", [P, 4, KEYS], F32, q)
                dT = sb("dT", [P, 4, S], F32, q)
            with ExitStack() as q:
                with ExitStack() as s:
                    gate = sb("gate", [P, 4, 2, NT, CW], F32, s)
                with ExitStack() as s:
                    m_hl = sb("m_hl", [P, 4, 2, 4, S], F32R, s)
                with ExitStack() as s:
                    krd = sb("krd", [P, NT, P], F32, s)
                    sb("over_gate0", [P, 2 * NT * CW - NT * P], F32, s)
                    cqT = sb("cqT", [P, 2, 4, S], F32R, s)
                    qnT = sb("qnT", [P, NH, S], F32, s)
                    qrT = sb("qrT", [P, NH // 2, S], F32, s)
                    ckvT = sb("ckvT", [P, 2, 2, S], F32R, s)
                sb("all_gates", [P, 4, 2, NT, CW], F32, q)
                qaT, kaT = sb("qaT", [P, 4, S], F32, q), sb("kaT", [P, 4, S], F32, q)
                va = sb("va", [P, NT, CW], F32, q)
                knT = sb("knT", [P, 2, 2, S], F32, q)
                vb = sb("vb", [P, 2, NT, 2 * HD], F32, q)
                krT = sb("krT", [P, 2, S], F32, q)
                rtmp = sb("rtmp", [P, 2, CW], F32, q)
        with ExitStack() as r:
            f_hi, f_lo = sb("f_hi", [P, FT, S], F32R, r), sb("f_lo", [P, FT, S], F32R, r)
        rows = stage[:, 0].rearrange("p a b -> p (a b)")
        junk = half_b.rearrange("p a b -> p (a b)")
        pbuf = half_a.rearrange("p a b -> p (a b)")[:, 0:2 * KEYS]
        pT = half_b.rearrange("p a b -> p (a b)")[:, 0:2 * KEYS]
        rel = half_a.rearrange("p a b -> p (a b)")
        fgain = halves[:].rearrange("p s a b -> p (s a b)")

        acc = [[ctx.enter_context(nc.psum_tensor(f"acc{g}{t}", [P, CW], F32)) for t in range(NT)] for g in range(2)]
        T = [ctx.enter_context(nc.psum_tensor(f"bank{b}", [P, CW], F32)) for b in range(4)]

        w_loaded = [sem(f"w_loaded{i}") for i in range(RING)]
        w_split_hi, w_split_lo, w_used = sem("w_split_hi"), sem("w_split_lo"), sem("w_used")
        acc_taken = [sem("acc_taken0"), sem("acc_taken1")]
        x_loaded = [sem(f"x_loaded{n}") for n in range(4)]
        const_loaded, ident_loaded, rows_loaded, taps_loaded, pool_loaded = (sem(n) for n in (
            "const_loaded", "ident_loaded", "rows_loaded", "taps_loaded", "pool_loaded"))
        fgain_loaded, stored = sem("fgain_loaded"), sem("stored")
        cols_turned, cols_ready, taps_turned, taps_ready = (sem(n) for n in ("cols_turned", "cols_ready", "taps_turned", "taps_ready"))
        kw_turned, kw_scaled = sem("kw_turned"), sem("kw_scaled")
        gqk_ready, premultiplied, angles, tables = sem("gqk_ready"), sem("premultiplied"), sem("angles"), sem("tables")
        consts_set, squared, mean_ready, rstd_ready = sem("consts_set"), sem("squared"), sem("mean_ready"), sem("rstd_ready")
        split_full, split_hi, split_lo = sem("split_full"), sem("split_hi"), sem("split_lo")
        copy_full, copy_done = sem("copy_full"), sem("copy_done")
        heads_mean, heads_rstd, heads_scaled, roped = sem("heads_mean"), sem("heads_rstd"), sem("heads_scaled"), sem("roped")
        rel_full, rel_done, isc_added = sem("rel_full"), sem("rel_done"), sem("isc_added")
        scores_full, scores_masked, exp_done, p_ready = sem("scores_full"), sem("scores_masked"), sem("exp_done"), sem("p_ready")
        lat_mean, lat_rstd = sem("lat_mean"), sem("lat_rstd")
        gates_open, mixed, kr_zeroed = sem("gates_open"), sem("mixed"), sem("kr_zeroed")
        conv_full, conv_seeded, conv_done, silu_done = sem("conv_full"), sem("conv_seeded"), sem("conv_done"), sem("silu_done")
        hidden, hidden_hi, f_ready = sem("hidden"), sem("hidden_hi"), sem("f_ready")
        dve_step, pool_step, normalised = sem("dve_step"), sem("pool_step"), sem("normalised")
        normalised_act = sem("normalised_act")

        block = ctx.enter_context(nc.Block())

        def weight_view(name, col, width, c):
            w = a[name]
            if name == "w_uq_2":
                v = w.rearrange("(c k p) (h e) -> c p k h e", p=P, k=KC, e=HD + ROPE_B)[c]
                if col < 2:
                    return [v[:, k, 4 * col:4 * col + 4, 0:HD] for k in range(KC)]
                return [v[:, k, :, HD:HD + ROPE_B] for k in range(KC)]
            v = w.rearrange("(c k p) n -> c p k n", p=P, k=KC_KW if width == KW else KC)[c]
            return [v[:, :, bass.ds(col, width)]]

        def in_slot(ring, slot, width):
            if width == KW:
                return ring[:, slot].rearrange("p k n -> p (k n)")[:, 0:KC_KW * KW]
            return ring[:, slot, :, 0:width]

        def with_loop(eng, counts, body, per):
            body(0)
            start = {k: c.now for k, c in counts.items()}
            with eng.Fori(1, PAIRS) as j:
                for k, c in counts.items():
                    c.now, c.i, c.per = start[k] - per[k], j, per[k]
                body(j)
                for k, c in counts.items():
                    assert c.now == start[k], (k, c.now, start[k], per[k])
            for k, c in counts.items():
                c.now, c.i, c.per = start[k] + per[k] * (PAIRS - 1), None, 0

        @block.sync
        def _(sp):
            chunk = Count()

            def load_x(n):
                sp.dma_start(x[:, :, n * CW:(n + 1) * CW],
                             a["x"][0].rearrange("(t p) d -> p t d", p=P)[:, :, n * CW:(n + 1) * CW]).then_inc(x_loaded[n], 16)

            def load(name, col, width, c):
                if chunk.now >= RING:
                    sp.wait_ge(w_split_lo, chunk.value(1 - RING))
                slot = chunk.now % RING
                views = weight_view(name, col, width, c)
                for k, v in enumerate(views):
                    if len(views) > 1:
                        d = w_raw[:, slot, k, 0:width]
                        d = d.rearrange("p (h e) -> p h e", h=v.shape[1])
                    else:
                        d = in_slot(w_raw, slot, width)
                        if width == KW:
                            d = d.rearrange("p (k n) -> p k n", n=KW)
                    sp.dma_start(d, v).then_inc(w_loaded[slot], 16)
                chunk.now += 1

            def pair(j, wa, ca, wb, cb):
                for w, c0 in ((wa, ca), (wb, cb)):
                    for c in range(KT // KC):
                        load(w, j * CW + c0, CW, c)

            sp.dma_start(ident[:], a["c_ident"]).then_inc(ident_loaded, 16)
            sp.dma_start(rows[0:G_ROWS, 0:P], a["gains"]).then_inc(rows_loaded, 16)
            g = 0
            while g < len(groups):
                if g == G_UP1:
                    with_loop(sp, {"chunk": chunk}, lambda j: pair(j, "w_up", 0, "w_up", DFF), {"chunk": 16})
                    g += 2 * PAIRS
                elif g == G_UP2:
                    with_loop(sp, {"chunk": chunk}, lambda j: pair(j, "w_gate_2", 0, "w_up_2", 0), {"chunk": 16})
                    g += 2 * PAIRS
                else:
                    name, col, width, ks, _ = groups[g]
                    for c in ks:
                        if chunk.now < 4:
                            load_x(chunk.now)
                        load(name, col, width, c)
                        if name == "w_down_2" and col == 0 and c == 16:
                            sp.dma_start(fgain, a["final_norm_2"].rearrange("(a n) -> a n", a=1).to_broadcast([P, D]))\
                              .then_inc(fgain_loaded, 16)
                    g += 1
            for t, h, by_vector, by_scalar in ((0, 0, 1, 0), (1, 0, 0, 1), (0, 1, 3, 0), (1, 1, 4, 2)):
                if by_vector:
                    sp.wait_ge(normalised, by_vector)
                if by_scalar:
                    sp.wait_ge(normalised_act, by_scalar)
                sp.dma_start(out[0, t * P:(t + 1) * P, h * 2 * CW:(h + 1) * 2 * CW],
                             x[:, t, h * 2 * CW:(h + 1) * 2 * CW]).then_inc(stored, 16)
            sp.wait_ge(stored, 16 * 2 * NT)

        @block.gpsimd
        def _(pool):
            pool.wait_ge(w_split_lo, 8)
            pool.dma_start(causal[:], a["c_causal"]).then_inc(const_loaded, 16)
            pool.dma_start(pool_m[:], a["c_pool"]).then_inc(const_loaded, 16)
            pool.dma_start(cos[:, 0, :], a["c_freq"]).then_inc(const_loaded, 16)
            pool.dma_start(pos_i[:], a["positions_2"][0, :].rearrange("(t p) -> p t", p=P),
                           allow_slow_non_contiguous=True).then_inc(const_loaded, 16)
            n_rstd, n_heads, n_roped, n_lat, steps = [0], [0], [0], [0], [0]

            def step(ins):
                steps[0] += 1
                ins.then_inc(pool_step, 1)

            def power(n):
                pool.wait_ge(mean_ready, n + 1)
                pool.tensor_tensor(rstd[:], meansq[:], minus_half[:, 0:NT], ALU.pow).then_inc(rstd_ready, 1)
            pool.wait_ge(consts_set, 1)

            def on_heads(kind, g):
                n_heads[0] += 1
                pool.wait_ge(heads_mean, n_heads[0])
                pool.tensor_tensor(hrstd[:].rearrange("p a b -> p (a b)"), hmean[:].rearrange("p a b -> p (a b)"),
                                   minus_half[:], ALU.pow).then_inc(heads_rstd, 1)

            def on_rstd():
                power(n_rstd[0])
                n_rstd[0] += 1

            def on_lat(kind):
                k = ("cq", "ckv").index(kind)
                n_lat[0] += 1
                pool.wait_ge(lat_mean, n_lat[0])
                pool.tensor_tensor(lrstd[:, k], lmean[:, k], minus_half[:, 0:NT], ALU.pow).then_inc(lat_rstd, 1)

            def on_rope(kind, g):
                pool.wait_ge(acc_taken[g % 2], 2 * (g // 2 + 1))
                pool.wait_ge(tables, 2)
                for t in range(NT):
                    st = stage[:, g % 2, t]
                    if kind == "a":
                        half, nh = ROPE_A // 2, 4
                        src = st.rearrange("p (h e) -> p h e", e=HD)[:, :, 0:ROPE_A]
                        f0 = 0
                    else:
                        half, nh = ROPE_B // 2, (1 if kind == "kr" else NH)
                        src = (st[:, 256:320] if kind == "kr" else st).rearrange("p (h e) -> p h e", e=ROPE_B)
                        f0 = 16
                    x1, x2 = src[:, :, 0:half], src[:, :, half:2 * half]
                    cs = cos[:, t, f0:f0 + half].unsqueeze(1).to_broadcast([P, nh, half])
                    sn = sin[:, t, f0:f0 + half].unsqueeze(1).to_broadcast([P, nh, half])
                    m = nh * half
                    tmp = [rtmp[:, k // 2, (k % 2) * 256:(k % 2) * 256 + m].rearrange("p (h e) -> p h e", h=nh) for k in range(4)]
                    if steps[0]:
                        pool.wait_ge(pool_step, steps[0])
                    step(pool.tensor_tensor(tmp[0], x1, cs, ALU.mult))
                    step(pool.tensor_tensor(tmp[1], x2, sn, ALU.mult))
                    step(pool.tensor_tensor(tmp[2], x2, cs, ALU.mult))
                    step(pool.tensor_tensor(tmp[3], x1, sn, ALU.mult))
                    pool.wait_ge(pool_step, steps[0])
                    if kind == "kr":
                        for d in range(2):
                            o1 = krd[:, t, d * 64:d * 64 + 32].unsqueeze(1)
                            o2 = krd[:, t, d * 64 + 32:d * 64 + 64].unsqueeze(1)
                            step(pool.tensor_tensor(o1, tmp[0], tmp[1], ALU.subtract))
                            step(pool.tensor_tensor(o2, tmp[2], tmp[3], ALU.add))
                    else:
                        step(pool.tensor_tensor(x1, tmp[0], tmp[1], ALU.subtract))
                        step(pool.tensor_tensor(x2, tmp[2], tmp[3], ALU.add))
                n_roped[0] += 1
                pool.wait_ge(pool_step, steps[0])
                pool.sem_inc(roped, 1)

            mine = {"headsq": on_heads, "rstd": on_rstd, "rstd0": on_rstd, "lat_rstd": on_lat, "rope": on_rope}
            for n in range(n_end + 8):
                for step_, *args in at.get(n, []):
                    if step_ == "isc" and args[0] == 5:
                        pool.wait_ge(rel_full, 6)
                        pool.dma_start(pool_w[:], a["pool_w"].rearrange("w (k p) d -> p w k d", p=P)).then_inc(pool_loaded, 16)
                    if step_ in mine:
                        mine[step_](*args)

        @block.tensor
        def _(pe):
            chunk, group, splits, copies = Count(), Count(), Count(), Count()
            rels, atts, convs, pvs, lats = Count(), Count(), Count(), [0], []
            roped_n, scaled_n, mix_n = [0], [0], [0]
            free = {}

            def wait_bank(*banks):
                for b in banks:
                    if b in free:
                        pe.wait_ge(*free[b])

            def turn(bank, pos, src, part=P):
                return pe.transpose(T[bank][:, pos:pos + part], src, ident[0:part, 0:part])

            def columns(c, k, width, operand, start, stop, g):
                hi, lo = operand
                slot = chunk.now % RING
                for t in range(NT):
                    o = acc[g][t][:, 0:width]
                    l, m = hi[:, t * P:(t + 1) * P], lo[:, t * P:(t + 1) * P]
                    pe.matmul(o, l, w_hi[:, slot, k, 0:width], start=start, stop=False)
                    pe.matmul(o, l, w_lo[:, slot, k, 0:width], start=False, stop=False)
                    last = pe.matmul(o, m, w_hi[:, slot, k, 0:width], start=False, stop=stop)
                return last

            def kw_columns(c, g):
                slot = chunk.now % RING
                hi, lo = in_slot(w_hi, slot, KW), in_slot(w_lo, slot, KW)
                for k in range(KC_KW):
                    kt = c * KC_KW + k
                    h, l, o = hi[:, k * KW:(k + 1) * KW], lo[:, k * KW:(k + 1) * KW], acc[g][0][0:KW, 0:S]
                    pe.matmul(o, h, xT_hi[:, kt], start=kt == 0, stop=False)
                    pe.matmul(o, h, xT_lo[:, kt], start=False, stop=False)
                    last = pe.matmul(o, l, xT_hi[:, kt], start=False, stop=kt == KT - 1)
                return last

            def stationary(kind, kt):
                if kind == "x":
                    return xT_hi[:, kt], xT_lo[:, kt]
                if kind in ("y", "ya"):
                    return y_hi[:, kt], y_lo[:, kt]
                if kind == "yb":
                    return y_hi[:, 8 + kt], y_lo[:, 8 + kt]
                if kind == "m":
                    return m_hl[:, kt // 4, 0, kt % 4], m_hl[:, kt // 4, 1, kt % 4]
                if kind == "f":
                    return f_hi[:, kt], f_lo[:, kt]
                if kind == "cq":
                    return cqT[:, 0, kt], cqT[:, 1, kt]
                return ckvT[:, 0, kt], ckvT[:, 1, kt]

            def stream(g, width, ks, kind, need=None, steps=None, table=True):
                if g is None or g >= 2:
                    pe.wait_ge(acc_taken[group.now % 2], 2 * group.turns(2))
                for c, kc in enumerate(ks):
                    if need and c in need:
                        pe.wait_ge(*need[c])
                    pe.wait_ge(w_split_lo, chunk.value(1))
                    for k in range(0 if kind == "kw" else KC):
                        last = columns(c, k, width, stationary(kind, kc * KC + k),
                                       c == 0 and k == 0, c == len(ks) - 1 and k == KC - 1, group.now % 2)
                    if kind == "kw":
                        last = kw_columns(c, group.now % 2)
                    last.then_inc(w_used, 1)
                    chunk.now += 1
                    if table:
                        run(chunk.now - 1)
                    if steps and c in steps:
                        steps[c]()
                group.now += 1

            def on_turn_taps():
                wait_bank(0)
                pe.wait_ge(taps_loaded, 16)
                for k in range(4):
                    last = turn(0, k * CT, rows[0:CT, (k + 1) * P:(k + 2) * P], CT)
                last.then_inc(taps_turned, 1)
                free[0] = (taps_ready, 1)

            def turn_kw(g):
                wait_bank(0)
                pe.wait_ge(acc_taken[g % 2], 2 * (g // 2 + 1))
                for t in range(NT):
                    last = turn(0, t * KW, stage[0:KW, g % 2, 0, t * P:(t + 1) * P], KW)
                last.then_inc(kw_turned, 1)
                free[0] = (kw_scaled, NT)

            def turn_ki():
                wait_bank(0)
                turn(0, 0, kdup[:, 0])
                turn(0, P, kdup[:, 1]).then_inc(copy_full, 1)
                copies.now += 1
                free[0] = (copy_done, copies.now)

            def four(bank, pick, done, n):
                for cc in range(2):
                    for t in range(NT):
                        last = turn(bank, cc * S + t * P, pick(cc, t))
                last.then_inc(done, 1)

            def turn_copy(name, g):
                if name in ("q1", "k1"):
                    scaled_n[0] += 1
                    pe.wait_ge(heads_scaled, scaled_n[0])
                elif name in ("qa", "ka", "qr"):
                    roped_n[0] += 1
                    pe.wait_ge(roped, roped_n[0])
                else:
                    pe.wait_ge(acc_taken[g % 2], 2 * (g // 2 + 1))
                for b in range(2):
                    wait_bank(b)
                    four(b, lambda cc, t: stage[:, g % 2, t, (2 * b + cc) * P:(2 * b + cc + 1) * P], copy_full, 1)
                    copies.now += 1
                    free[b] = (copy_done, copies.now)

            def on_rel(u):
                wait_bank(2, 3)
                pe.wait_ge(copy_done, 5)
                blk, h0, nh, nk = rel_unit(u)
                for k in range(nh):
                    h = h0 + k
                    r = IDX_DIM * (h % 2)
                    last = pe.matmul(T[2 + h % 2][:, (k // 2) * nk:(k // 2 + 1) * nk],
                                     qiT[r:r + IDX_DIM, h // 2, blk * P:(blk + 1) * P],
                                     kiT[r:r + IDX_DIM, 0:nk], start=True, stop=True)
                last.then_inc(rel_full, 1)
                rels.now += 1
                free[2] = free[3] = (rel_done, rels.now)

            def operands(which, pair, j):
                if which == "one":
                    return q1T[:, 2 * pair + j], k1T[:, 2 * pair + j], v1[:, :, (2 * pair + j) * HD:(2 * pair + j + 1) * HD]
                if which == "moba":
                    h = 2 * (pair % 2) + j
                    return qaT[:, h], kaT[:, h], va[:, :, h * HD:(h + 1) * HD]
                return qnT[:, 2 * pair + j], knT[:, pair % 2, j], vb[:, pair % 2, :, j * HD:(j + 1) * HD]

            def on_scores(which, pair):
                wait_bank(2, 3)
                pe.wait_ge(copy_done, copies.now)
                for blk in range(2):
                    nk = P * (blk + 1)
                    for j in range(2):
                        q, k, _ = operands(which, pair, j)
                        o = T[2 + blk][:, j * nk:(j + 1) * nk]
                        last = pe.matmul(o, q[:, blk * P:(blk + 1) * P], k[:, 0:nk], start=True, stop=which != "mla")
                        if which == "mla":
                            last = pe.matmul(o, qrT[:, pair, blk * P:(blk + 1) * P], krT[:, j, 0:nk],
                                             start=False, stop=True)
                last.then_inc(scores_full, 1)
                atts.now += 1
                free[2] = free[3] = (scores_masked, atts.now)

            def on_turn_p(which):
                wait_bank(0, 1)
                pe.wait_ge(p_ready, atts.now)
                for j in range(2):
                    turn(0, j * S, pbuf[:, j * P:(j + 1) * P])
                    last = turn(0, j * S + P, pbuf[:, S + j * S:S + j * S + P])
                last.then_inc(copy_full, 1)
                for j in range(2):
                    last = turn(1, j * P, pbuf[:, S + j * S + P:S + (j + 1) * S])
                last.then_inc(copy_full, 1)
                copies.now += 2
                free[0], free[1] = (copy_done, copies.now - 1), (copy_done, copies.now)
                pvs[0] = copies.now

            def on_pv(which, pair):
                wait_bank(2)
                pe.wait_ge(copy_done, pvs[0])
                for j in range(2):
                    v = operands(which, pair, j)[2]
                    pe.matmul(T[2][:, j * S:(j + 1) * S], v[:, 0], pT[:, j * S:(j + 1) * S], start=True, stop=False)
                    last = pe.matmul(T[2][:, j * S + P:(j + 1) * S], v[:, 1], pT[:, 2 * S + j * P:2 * S + (j + 1) * P],
                                     start=False, stop=True)
                last.then_inc(split_full, 1)
                splits.now += 1
                free[2] = (split_lo, splits.now)

            def on_pool_d(n, g):
                pe.wait_ge(const_loaded, 16 * 4)
                wait_bank(0, 1)
                pe.wait_ge(acc_taken[g % 2], 2 * (g // 2 + 1))
                for cc in range(4):
                    o, w = T[cc // 2][:, (cc % 2) * S:(cc % 2 + 1) * S], 2 * n + cc // 2
                    st = stage[:, g % 2, :, cc * P:(cc + 1) * P]
                    pe.matmul(o, st[:, 0], pool_m[:, w, 0:S], start=True, stop=False)
                    last = pe.matmul(o[:, P:S], st[:, 1], pool_m[:, w, S:KEYS], start=False, stop=True)
                    if cc % 2:
                        last.then_inc(copy_full, 1)
                        copies.now += 1
                        free[cc // 2] = (copy_done, copies.now)

            def on_pool_y(n):
                wait_bank(2, 3)
                pe.wait_ge(copy_done, copies.now)
                pe.wait_ge(pool_loaded, 16)
                for w in range(2):
                    for dc in range(2):
                        o = T[2 + w][:, dc * S:(dc + 1) * S]
                        for cc in range(2):
                            last = pe.matmul(o, pool_w[:, 2 * n + w, cc, dc * P:(dc + 1) * P], dT[:, 2 * w + cc],
                                             start=cc == 0, stop=cc == 1)
                    last.then_inc(split_full, 1)
                    splits.now += 1
                    free[2 + w] = (split_lo, splits.now)

            def on_turn_x(n, g):
                pe.wait_ge(acc_taken[g % 2], 2 * (g // 2 + 1))
                for b in range(2):
                    wait_bank(b)
                    four(b, lambda cc, t: x[:, t, n * CW + (2 * b + cc) * P:n * CW + (2 * b + cc + 1) * P], split_full, 1)
                    splits.now += 1
                    free[b] = (split_lo, splits.now)

            def on_turn_stage(g, banks, wait):
                pe.wait_ge(*wait)
                for b in banks:
                    wait_bank(b)
                    four(b, lambda cc, t: stage[:, g % 2, t, (2 * b + cc) * P:(2 * b + cc + 1) * P], split_full, 1)
                    splits.now += 1
                    free[b] = (split_lo, splits.now)

            def on_turn_lat(kind, g):
                on_turn_stage(g, range(2 if kind == "cq" else 1), (acc_taken[g % 2], 2 * (g // 2 + 1)))
                lats.append(splits.now)

            def on_turn_mix(g):
                mix_n[0] += 1
                on_turn_stage(0, range(2), (mixed, mix_n[0]))

            def on_turn_kr():
                wait_bank(0)
                roped_n[0] += 1
                pe.wait_ge(roped, roped_n[0])
                turn(0, 0, krd[:, 0])
                turn(0, P, krd[:, 1]).then_inc(copy_full, 1)
                copies.now += 1
                free[0] = (copy_done, copies.now)

            def on_turn_kn(k, g):
                wait_bank(0)
                pe.wait_ge(acc_taken[g % 2], 2 * (g // 2 + 1))
                four(0, lambda cc, t: stage[:, g % 2, t, 2 * cc * P:(2 * cc + 1) * P], copy_full, 1)
                copies.now += 1
                free[0] = (copy_done, copies.now)

            mine = {"turn_taps": on_turn_taps, "turn_kw": turn_kw, "turn_ki": turn_ki, "turn_copy": turn_copy, "rel": on_rel, "scores": on_scores,
                    "turn_p": on_turn_p, "pv": on_pv, "pool_d": on_pool_d, "pool_y": on_pool_y,
                    "turn_x": on_turn_x, "turn_lat": on_turn_lat, "turn_mix": on_turn_mix,
                    "turn_kr": on_turn_kr, "turn_kn": on_turn_kn}

            def run(n):
                for step_, *args in at.get(n, []):
                    if step_ in mine:
                        mine[step_](*args)

            pe.wait_ge(rows_loaded, 16)
            pe.wait_ge(ident_loaded, 16)
            turn(0, 0, rows[0:G_ROWS, 0:P], G_ROWS).then_inc(cols_turned, 1)
            free[0] = (cols_ready, 1)

            def turn_input(n):
                pe.wait_ge(x_loaded[n], 16)
                for m in (2 * n, 2 * n + 1):
                    b = (m + 1) % 4
                    wait_bank(b)
                    four(b, lambda cc, t: x[:, t, (2 * m + cc) * P:(2 * m + cc + 1) * P], split_full, 1)
                    splits.now += 1
                    free[b] = (split_lo, splits.now)

            turn_input(0)
            turn_input(1)

            def turned(par, banks, done):
                for b in banks:
                    four(b, lambda cc, t: stage[:, par, t, (2 * (b % 2) + cc) * P:(2 * (b % 2) + cc + 1) * P], done, 1)

            def taken_before(par):
                pe.wait_ge(acc_taken[par], 2 * group.turns(2, -1) + 2)

            def turn_conv(par, banks, first=False):
                taken_before(par)
                if first:
                    wait_bank(*banks)
                else:
                    pe.wait_ge(conv_done, convs.value())
                turned(par, banks, conv_full)
                convs.now += 2

            def turn_product(par):
                taken_before(par)
                pe.wait_ge(split_lo, splits.value())
                turned(0, (0, 1), split_full)
                splits.now += 2

            def feed_forward(layer, need):
                par = group.now % 2
                whole = list(range(KT // KC))

                def pair(j):
                    first = isinstance(j, int)
                    if layer == 1:
                        gate_steps = {} if first else {1: lambda: turn_conv(1 - par, (2, 3))}
                        value_steps = {1: lambda: turn_conv(par, (0, 1), first)}
                    else:
                        gate_steps, value_steps = {} if first else {1: lambda: turn_product(1 - par)}, {}
                    stream(None, CW, whole, "x", need if first else None, gate_steps, first)
                    stream(None, CW, whole, "x", None, value_steps, first)
                if layer == 1:
                    wait_bank(2, 3)
                counts = {"chunk": chunk, "group": group, "splits": splits, "convs": convs}
                per = {"chunk": 16, "group": 2, "splits": 0 if layer == 1 else 2,
                       "convs": 4 if layer == 1 else 0}
                with_loop(pe, counts, pair, per)
                return {1: lambda: turn_conv(1 - par, (2, 3)) if layer == 1 else turn_product(1 - par)}

            g, steps = 0, None
            while g < len(groups):
                name, col, width, ks, kind = groups[g]
                now, need = splits.now, {}
                if g == 0:
                    need = {c: (split_lo, c + 1) for c in range(8)}
                    steps = {0: lambda: turn_input(2), 1: lambda: turn_input(3)}
                elif name == "w_out" and col == 0:
                    need = {0: (split_lo, 13), 5: (split_lo, 14), 6: (split_lo, 15), 7: (split_lo, 16)}
                elif g in (G_UP1, G_UP2, G_IN2) or name == "w_out_2" and col == 0:
                    need = {0: (split_lo, now), 6: (split_lo, now + 1), 7: (split_lo, now + 2)}
                elif name == "w_down" and col == 0:
                    need = {c: (f_ready, c // 2 + 1) for c in range(0, FT // KC, 2)}
                elif name == "w_down_2" and col == 0:
                    need = {c: (split_lo, now - 2 * (PAIRS - 1) + c + 1) for c in range(FT // KC)}
                elif name == "w_uq_2" and col == 0:
                    need = {0: (split_lo, lats[0])}
                elif name == "w_ukv_2" and col == 0:
                    need = {0: (split_lo, lats[1])}
                elif name == "w_branch_a_2" and col == 0:
                    need = {0: (split_lo, now)}
                if g in (G_UP1, G_UP2):
                    steps = feed_forward(1 if g == G_UP1 else 2, need)
                    g += 2 * PAIRS
                else:
                    stream(g, width, ks, kind, need, steps)
                    steps = None
                    g += 1
            for n in range(n_end, n_end + 8):
                run(n)

        @block.scalar
        def _(act):
            chunk, loads = Count(), [Count() for _ in range(RING)]
            splits, copies, convs, hiddens = Count(), Count(), Count(), Count()
            n_rstd, n_squared, n_att, n_rel = [0], [0], [0], [0]

            def split(name, width):
                slot = chunk.now % RING
                loads[slot].now += 2 if name == "w_uq_2" else 1
                act.wait_ge(w_loaded[slot], loads[slot].sixteens())
                if chunk.per or chunk.now >= RING:
                    act.wait_ge(w_used, chunk.value(1 - RING))
                act.activation(in_slot(w_hi, slot, width), in_slot(w_raw, slot, width), ACT.Copy).then_inc(w_split_hi, 1)
                chunk.now += 1

            def finished(g):
                act.wait_ge(w_used, first[g] + len(groups[g][3]))

            def taken(g):
                return acc_taken[g % 2], 2 * (g // 2 + 1)

            def on_evac(kind, g, *dest):
                finished(g)
                name, _, width, _, _ = groups[g]
                act.wait_ge(rstd_ready, n_rstd[0])
                if name in ("w_uq_2", "w_ukv_2"):
                    act.wait_ge(lat_rstd, 2)
                for t in range(NT):
                    scale = rstd[:, t:t + 1]
                    if name in ("w_uq_2", "w_ukv_2"):
                        k = 0 if name == "w_uq_2" else 1
                        scale = lrstd[:, k, t:t + 1]
                    src = acc[g % 2][t][:, 0:width]
                    if kind == "v":
                        o = v1[:, t, dest[1] * CW:(dest[1] + 1) * CW]
                    elif kind == "va":
                        o = va[:, t]
                    elif kind == "gate":
                        o = gate[:, dest[1], dest[0], t]
                    else:
                        o = stage[:, g % 2, t, 0:width]
                    if kind == "ukv":
                        act.activation(vb[:, dest[0] % 2, t].rearrange("p (h e) -> p h e", h=2),
                                       src.rearrange("p (h a e) -> p h a e", h=2, a=2)[:, :, 1], ACT.Copy, scale=scale)
                        o = o.rearrange("p (h a e) -> p h a e", h=2, a=2)[:, :, 0]
                        src = src.rearrange("p (h a e) -> p h a e", h=2, a=2)[:, :, 0]
                    act.activation(o, src, ACT.Copy, scale=scale).then_inc(acc_taken[g % 2], 1)

            def copied(out_, bank, width=CW, scale=1.0):
                copies.now += 1
                act.wait_ge(copy_full, copies.now)
                act.activation(out_, T[bank][:, 0:width], ACT.Copy, scale=scale).then_inc(copy_done, 1)

            def on_copy_kw(g):
                finished(g)
                for t in range(NT):
                    act.activation(stage[0:KW, g % 2, 0, t * P:(t + 1) * P], acc[g % 2][0][0:KW, t * P:(t + 1) * P],
                                   ACT.Copy).then_inc(acc_taken[g % 2], 1)

            def on_copy_ki():
                copied(kiT[:], 0, S)

            def on_copy2(name, half):
                act.wait_ge(gqk_ready, 1)
                for b in range(2):
                    dest, k = {"qi": (qiT, 4), "q1": (q1T, 4), "k1": (k1T, 4), "qa": (qaT, 0), "ka": (kaT, 0),
                               "qn": (qnT, 4), "qr": (qrT, 0)}[name]
                    scale = {"k1": gqk[:], "qa": HD ** -0.5, "qn": (HD + ROPE_B) ** -0.5, "qr": (HD + ROPE_B) ** -0.5}.get(name, 1.0)
                    o = dest[:, k * half + 2 * b:k * half + 2 * b + 2].rearrange("p a b -> p (a b)")
                    copied(o, b, CW, scale)

            def on_relu(u):
                n_rel[0] += 1
                act.wait_ge(rel_full, n_rel[0])
                if n_rel[0] > 1:
                    act.wait_ge(isc_added, n_rel[0] - 1)
                act.activation(rel[:, 0:CW], T[2][:], ACT.Relu)
                act.activation(rel[:, CW:2 * CW], T[3][:], ACT.Relu).then_inc(rel_done, 1)

            def on_exp(which):
                n_att[0] += 1
                act.wait_ge(scores_masked, n_att[0])
                for k in range(4):
                    blk, j = k // 2, k % 2
                    nk = P * (blk + 1)
                    v = pbuf[:, blk * S + j * nk:blk * S + (j + 1) * nk]
                    last = act.activation(v, v, ACT.Exp, bias=negmax[:, k:k + 1], accum_out=psum_[:, k:k + 1])
                last.then_inc(exp_done, 1)

            def on_copy_p(which):
                copied(pT[:, 0:2 * S], 0)
                copied(pT[:, 2 * S:3 * S], 1, S)

            def on_copy_d(n):
                for b in range(2):
                    copied(dT[:, 2 * b:2 * b + 2].rearrange("p a b -> p (a b)"), b)

            def on_copy_kr():
                copies.now += 1
                act.wait_ge(copy_full, copies.now)
                act.wait_ge(kr_zeroed, 1)
                act.activation(krT[0:64, 0], T[0][0:64, 0:S], ACT.Copy)
                act.activation(krT[64:128, 1], T[0][64:128, 0:S], ACT.Copy).then_inc(copy_done, 1)

            def on_copy_kn(k):
                copied(knT[:, k % 2].rearrange("p a b -> p (a b)"), 0)

            def high(outs, bank, gain=None):
                splits.now += 1
                act.wait_ge(split_full, splits.now)
                n = len(outs)
                for k, o in enumerate(outs):
                    w = CW // n
                    scale = 1.0 if gain is None else cols[:, gain + k:gain + k + 1]
                    last = act.activation(o, T[bank][:, k * w:(k + 1) * w], ACT.Copy, scale=scale)
                last.then_inc(split_hi, 1)

            def on_split_y(which, pair):
                k = 2 * pair + (0 if which == "moba" else 8)
                high([y_hi[:, k:k + 2].rearrange("p a b -> p (a b)")], 2)

            def on_split_x(n, gain, b):
                k = 4 * n + 2 * b
                high([xT_hi[:, k], xT_hi[:, k + 1]], b, gain + k)

            def on_split_pool(n):
                for w in range(2):
                    k = 4 * n + 2 * w
                    high([y_hi[:, k], y_hi[:, k + 1]], 2 + w, G_POOL + k)

            def on_split_lat(kind):
                o, gain = (cqT, G_CQ) if kind == "cq" else (ckvT, G_CKV)
                for b in range(2 if kind == "cq" else 1):
                    high([o[:, 0, 2 * b], o[:, 0, 2 * b + 1]], b, gain + 2 * b)

            def on_split_mix(n):
                for b in range(2):
                    high([m_hl[:, n, 0, 2 * b:2 * b + 2].rearrange("p a b -> p (a b)")], b)

            def square(src, k, dest, last_layer=False):
                if n_squared[0]:
                    act.wait_ge(squared, n_squared[0])
                bin_ = T[2 + k][:] if last_layer else junk[:, k * CW:(k + 1) * CW]
                act.activation(bin_[:, 0:src.shape[1]], src, ACT.Square, accum_out=dest).then_inc(squared, 1)
                n_squared[0] += 1

            def on_square(g, n):
                for t in range(NT):
                    act.wait_ge(acc_taken[g % 2], 2 * (g // 2) + t + 1)
                    square(x[:, t, n * CW:(n + 1) * CW], t, sumsq[:, t, n:n + 1], g > G_UP2)

            def on_lat_square(kind, g):
                act.wait_ge(*taken(g))
                k, w = (0, 512) if kind == "cq" else (1, 256)
                for t in range(NT):
                    square(stage[:, g % 2, t, 0:w], t, lsum[:, k, t:t + 1])

            def on_square0(n):
                for t in range(NT):
                    square(x[:, t, n * CW:(n + 1) * CW], t, sumsq[:, t, n:n + 1])

            def on_rstd():
                n_rstd[0] += 1

            def on_copy_taps():
                act.wait_ge(taps_turned, 1)
                act.activation(cols[:, CONV_COL:CONV_COL + 4 * CT], T[0][:, 0:4 * CT], ACT.Copy).then_inc(taps_ready, 1)

            def on_angles():
                act.wait_ge(angles, 1)
                act.activation(sin[:], sin[:], ACT.Sin).then_inc(tables, 1)
                act.activation(cos[:], cos[:], ACT.Sin).then_inc(tables, 1)

            def on_sigmoid(n):
                for k in range(2):
                    act.wait_ge(acc_taken[k], last_gate[k])
                v = gate[:, n].rearrange("p a b c -> p (a b c)")
                act.activation(v, v, ACT.Sigmoid).then_inc(gates_open, 1)

            mine = {"evac": on_evac, "copy_kw": on_copy_kw, "copy_ki": on_copy_ki, "copy2": on_copy2, "relu": on_relu, "exp": on_exp,
                    "copy_p": on_copy_p, "copy_d": on_copy_d, "copy_kr": on_copy_kr, "copy_kn": on_copy_kn,
                    "split_y": on_split_y, "split_x": on_split_x, "split_pool": on_split_pool,
                    "split_lat": on_split_lat, "split_mix": on_split_mix, "square": on_square,
                    "lat_square": on_lat_square, "rstd": on_rstd, "sigmoid": on_sigmoid,
                    "square0": on_square0, "rstd0": on_rstd, "copy_taps": on_copy_taps, "angles": on_angles}

            def run(n):
                for step_, *args in at.get(n, []):
                    if step_ in mine:
                        mine[step_](*args)

            act.dma_start(rows[0:CT, P:5 * P].rearrange("p (k c) -> p k c", c=P),
                          a["taps"].rearrange("k (r c) -> r k c", c=P)).then_inc(taps_loaded, 16)
            act.wait_ge(cols_turned, 1)
            act.activation(cols[:, 0:G_ROWS], T[0][:, 0:G_ROWS], ACT.Copy).then_inc(cols_ready, 1)
            act.wait_ge(cols_ready, 1)
            for m in range(KT // 2):
                high([xT_hi[:, 2 * m], xT_hi[:, 2 * m + 1]], (m + 1) % 4, G_ATTN1 + 2 * m)
                if m % 2:
                    split("w_in", groups[0][2])

            def evac_hidden(par):
                act.wait_ge(w_used, chunk.value(-LEAD - 1))
                act.wait_ge(rstd_ready, n_rstd[0])
                for t in range(NT):
                    act.activation(stage[:, par, t], acc[par][t][:], ACT.Copy, scale=rstd[:, t:t + 1]).then_inc(acc_taken[par], 1)

            def seed(bank, dest, j, base):
                convs.now += 1
                act.wait_ge(taps_ready, 1)
                act.wait_ge(conv_full, convs.value())
                for cc in range(2):
                    k = CONV_COL + base + 2 * (bank % 2) + cc
                    last = act.activation(dest[:, 2 * (bank % 2) + cc], T[bank][:, cc * S:(cc + 1) * S], ACT.Identity,
                                          scale=cols[:, bass.ds(j * 4 + (k + 2 * CT), 1)],
                                          bias=cols[:, bass.ds(j * 4 + (k + 3 * CT), 1)])
                last.then_inc(conv_seeded, 1)

            def silu():
                act.wait_ge(conv_done, convs.value())
                act.activation(half_a, half_a, ACT.Silu).then_inc(silu_done, 1)

            def hidden_high(j):
                hiddens.now += 1
                act.wait_ge(hidden, hiddens.value())
                act.activation(f_hi[:, bass.ds(j * 4, 4)], half_b, ACT.Copy).then_inc(hidden_hi, 1)

            def gate_silu(par):
                act.wait_ge(w_used, chunk.value(-LEAD - 1))
                act.wait_ge(rstd_ready, n_rstd[0])
                for t in range(NT):
                    act.activation(half_a.rearrange("p (t a) b -> p t (a b)", t=NT)[:, t], acc[par][t][:], ACT.Silu,
                                   scale=rstd[:, t:t + 1]).then_inc(acc_taken[par], 1)

            def product_high(j):
                for b in range(2):
                    splits.now += 1
                    act.wait_ge(split_full, splits.value())
                    act.activation(f_hi[:, bass.ds(j * 4 + 2 * b, 2)].rearrange("p a b -> p (a b)"), T[b][:], ACT.Copy).then_inc(split_hi, 1)

            def feed_forward(layer, g0):
                par = g0 % 2

                def value_steps(j):
                    if layer == 1:
                        return {0: lambda: evac_hidden(1 - par), 2: lambda: seed(2, half_b, j, FT),
                                3: lambda: seed(3, half_b, j, FT), 5: lambda: hidden_high(j)}
                    return {2: lambda: product_high(j)}

                def pair(j):
                    first_ = isinstance(j, int)
                    steps = {} if first_ else value_steps(j - 1)
                    if layer == 1:
                        steps.update({8: lambda: evac_hidden(par), 10: lambda: seed(0, half_a, j, 0),
                                      11: lambda: seed(1, half_a, j, 0), 12: silu})
                    else:
                        steps.update({8: lambda: gate_silu(par)})
                    for c in range(2 * KT // KC):
                        split("w_up", CW)
                        if first_:
                            run(chunk.now - 1 - LEAD)
                        if c - LEAD in steps:
                            steps[c - LEAD]()
                counts = {"chunk": chunk, "splits": splits, "convs": convs, "hiddens": hiddens}
                counts.update({f"load{k}": loads[k] for k in range(RING)})
                per = {"chunk": 16, "splits": 0 if layer == 1 else 2, "convs": 4 if layer == 1 else 0,
                       "hiddens": 1 if layer == 1 else 0}
                per.update({f"load{k}": 16 // RING for k in range(RING)})
                with_loop(act, counts, pair, per)
                return value_steps(PAIRS - 1)

            last_gate = [max(2 * (g // 2 + 1) for g in gate_groups if g % 2 == k) for k in range(2)]
            g, steps = 0, {}
            while g < len(groups):
                if g in (G_UP1, G_UP2):
                    steps = feed_forward(1 if g == G_UP1 else 2, g)
                    g += 2 * PAIRS
                    continue
                name, _, width, ks, _ = groups[g]
                for c in range(len(ks)):
                    if chunk.now < first[g] + c + 1:
                        split(name, width)
                    if chunk.now - 1 - LEAD >= 0:
                        run(first[g] + c - LEAD)
                    if c - LEAD in steps:
                        steps[c - LEAD]()
                steps = {}
                g += 1
            for n in range(n_end - LEAD, n_end + 8):
                run(n)
            act.wait_ge(rstd_ready, 5)
            act.wait_ge(premultiplied, 6)
            for lo_, hi_ in ((0, 2 * CW), (2 * CW, 3 * CW)):
                v = x[:, 1, lo_:hi_]
                act.activation(v, v, ACT.Copy, scale=rstd[:, 1:2]).then_inc(normalised_act, 1)

        @block.vector
        def _(dve):
            chunk = Count()
            step_n, splits, convs, seeds, hiddens, silus = Count(), Count(), Count(), Count(), Count(), Count()
            n_squared, n_att, n_rel, n_heads = [0], [0], [0], [0]

            def link(ins):
                ins.then_inc(dve_step, 1)
                step_n.now += 1

            def linked():
                dve.wait_ge(dve_step, step_n.value())

            def split(width):
                slot = chunk.now % RING
                chunk.now += 1
                dve.wait_ge(w_split_hi, chunk.value())
                dve.tensor_tensor(in_slot(w_lo, slot, width), in_slot(w_raw, slot, width),
                                  in_slot(w_hi, slot, width).bitcast(F32), ALU.subtract).then_inc(w_split_lo, 1)

            def finished(g):
                dve.wait_ge(w_used, first[g] + len(groups[g][3]))

            def on_evac_kw():
                dve.wait_ge(kw_turned, 1)
                dve.wait_ge(rstd_ready, 1)
                for t in range(NT):
                    r, key = rstd[:, t:t + 1], T[0][:, t * KW:t * KW + IDX_DIM]
                    dve.tensor_scalar(widx[:, t], T[0][:, t * KW + IDX_DIM:(t + 1) * KW], r, 2.0 ** -5, ALU.mult, ALU.mult)
                    dve.tensor_scalar(kdup[:, t, 0:64], key, r, None, ALU.mult)
                    dve.tensor_scalar(kdup[:, t, 64:128], key, r, None, ALU.mult).then_inc(kw_scaled, 1)

            def on_headsq(name, g):
                dve.wait_ge(acc_taken[g % 2], 2 * (g // 2 + 1))
                for t in range(NT):
                    st = stage[:, g % 2, t]
                    if step_n.now:
                        linked()
                    link(dve.tensor_tensor(hsq[:], st, st, ALU.mult))
                    linked()
                    link(dve.tensor_reduce(hsum[:, t], hsq[:].rearrange("p (h e) -> p h e", h=4), AX.X, ALU.add))
                linked()
                mul, add = (1.0, HD * EPS) if name == "q1" else (1.0 / HD, EPS)
                dve.tensor_scalar(hmean[:], hsum[:], mul, add, ALU.mult, ALU.add).then_inc(heads_mean, 1)

            def on_headscale(name, g):
                n_heads[0] += 1
                dve.wait_ge(heads_rstd, n_heads[0])
                for t in range(NT):
                    st = stage[:, g % 2, t].rearrange("p (h e) -> p h e", h=4)
                    last = dve.tensor_tensor(st, st, hrstd[:, t].unsqueeze(2).to_broadcast([P, 4, HD]), ALU.mult)
                last.then_inc(heads_scaled, 1)

            def on_isc(u):
                n_rel[0] += 1
                dve.wait_ge(rel_done, n_rel[0])
                blk, h0, nh, nk = rel_unit(u)
                o = isc[:, blk * P:blk * P + nk]
                for k in range(nh):
                    r = rel[:, (k % 2) * CW + (k // 2) * nk:(k % 2) * CW + (k // 2 + 1) * nk]
                    w = widx[:, blk, h0 + k:h0 + k + 1]
                    if h0 + k == 0:
                        last = dve.tensor_scalar(o, r, w, None, ALU.mult)
                    else:
                        linked()
                        last = dve.scalar_tensor_tensor(o, r, w, o, ALU.mult, ALU.add)
                    link(last)
                linked()
                dve.sem_inc(isc_added, 1)

            def on_topk(r):
                if r == 0:
                    dve.wait_ge(const_loaded, 16 * 4)
                    link(dve.tensor_tensor(isc[:], isc[:], causal[:], ALU.min))
                linked()
                src = isc[:] if r == 0 else picked[:, (r - 1) % 2]
                spans = ((0, P), (P, KEYS))
                for k, (lo_, hi_) in enumerate(spans):
                    link(dve.max(top8[:, k], src[:, lo_:hi_]))
                linked()
                for k, (lo_, hi_) in enumerate(spans):
                    link(dve.match_replace(picked[:, r % 2, lo_:hi_], top8[:, k], src[:, lo_:hi_], FMIN))

            def on_select():
                linked()
                link(dve.tensor_tensor(sel[:], picked[:, (TOPK // 8 - 1) % 2], isc[:], ALU.is_lt))
                linked()
                link(dve.tensor_scalar(sel[:], sel[:], 0.5, BIG, ALU.subtract, ALU.mult))

            def on_mask(which):
                n_att[0] += 1
                dve.wait_ge(scores_full, n_att[0])
                m = sel if which == "one" else causal
                if which == "one":
                    linked()
                for blk in range(2):
                    nk = P * (blk + 1)
                    v = pbuf[:, blk * S:blk * S + 2 * nk].rearrange("p (j n) -> p j n", j=2)
                    link(dve.tensor_tensor(v, T[2 + blk][:, 0:2 * nk].rearrange("p (j n) -> p j n", j=2),
                                           m[:, blk * P:blk * P + nk].unsqueeze(1).to_broadcast([P, 2, nk]), ALU.min))
                linked()
                for blk in range(2):
                    nk = P * (blk + 1)
                    v = pbuf[:, blk * S:blk * S + 2 * nk].rearrange("p (j n) -> p j n", j=2)
                    last = dve.tensor_reduce(negmax[:, 2 * blk:2 * blk + 2], v, AX.X, ALU.max, negate=True)
                last.then_inc(scores_masked, 1)

            def on_norm(which):
                dve.wait_ge(exp_done, n_att[0])
                link(dve.reciprocal(pinv[:], psum_[:]))
                linked()
                for blk in range(2):
                    nk = P * (blk + 1)
                    v = pbuf[:, blk * S:blk * S + 2 * nk].rearrange("p (j n) -> p j n", j=2)
                    last = dve.tensor_tensor(v, v, pinv[:, 2 * blk:2 * blk + 2].unsqueeze(2).to_broadcast([P, 2, nk]), ALU.mult)
                last.then_inc(p_ready, 1)

            def low(outs, his, bank, gain=None):
                splits.now += 1
                dve.wait_ge(split_hi, splits.now)
                n = len(outs)
                for k, (o, h) in enumerate(zip(outs, his)):
                    w = CW // n
                    b = T[bank][:, k * w:(k + 1) * w]
                    if gain is None:
                        last = dve.tensor_tensor(o, b, h.bitcast(F32), ALU.subtract)
                    else:
                        last = dve.scalar_tensor_tensor(o, b, cols[:, gain + k:gain + k + 1], h.bitcast(F32),
                                                        ALU.mult, ALU.subtract)
                last.then_inc(split_lo, 1)

            def on_split_y(which, pair):
                k = 2 * pair + (0 if which == "moba" else 8)
                low([y_lo[:, k:k + 2].rearrange("p a b -> p (a b)")], [y_hi[:, k:k + 2].rearrange("p a b -> p (a b)")], 2)

            def on_split_x(n, gain, b):
                k = 4 * n + 2 * b
                low([xT_lo[:, k], xT_lo[:, k + 1]], [xT_hi[:, k], xT_hi[:, k + 1]], b, gain + k)

            def on_split_pool(n):
                for w in range(2):
                    k = 4 * n + 2 * w
                    low([y_lo[:, k], y_lo[:, k + 1]], [y_hi[:, k], y_hi[:, k + 1]], 2 + w, G_POOL + k)

            def on_split_lat(kind):
                o, gain = (cqT, G_CQ) if kind == "cq" else (ckvT, G_CKV)
                for b in range(2 if kind == "cq" else 1):
                    low([o[:, 1, 2 * b], o[:, 1, 2 * b + 1]], [o[:, 0, 2 * b], o[:, 0, 2 * b + 1]], b, gain + 2 * b)

            def on_split_mix(n):
                for b in range(2):
                    v = m_hl[:, n, :, 2 * b:2 * b + 2].rearrange("p s a b -> p s (a b)")
                    low([v[:, 1]], [v[:, 0]], b)

            def on_res(g, n):
                finished(g)
                for t in range(NT):
                    v = x[:, t, n * CW:(n + 1) * CW]
                    dve.tensor_tensor(v, acc[g % 2][t][:], v, ALU.add).then_inc(acc_taken[g % 2], 1)

            def mean(sums):
                dve.wait_ge(squared, sums)
                link(dve.tensor_reduce(meansq[:], sumsq[:], AX.X, ALU.add))
                linked()
                dve.tensor_scalar(meansq[:], meansq[:], 1.0 / D, EPS, ALU.mult, ALU.add).then_inc(mean_ready, 1)

            def on_angles():
                ang, turns_, r_ = (rel[:, k * 128:k * 128 + 96].rearrange("p (t f) -> p t f", t=NT) for k in range(3))
                dve.wait_ge(const_loaded, 16 * 4)
                link(dve.tensor_copy(pos_f[:], pos_i[:])); linked()
                for t in range(NT):
                    link(dve.tensor_scalar(ang[:, t], cos[:, 0], pos_f[:, t:t + 1], None, ALU.mult))
                linked()
                link(dve.tensor_scalar(turns_, ang, 1.0 / (2 * math.pi), ROUND, ALU.mult, ALU.add)); linked()
                link(dve.tensor_scalar(turns_, turns_, ROUND, None, ALU.subtract)); linked()
                src = ang
                for c in TWO_PI:
                    link(dve.scalar_tensor_tensor(r_, turns_, -c, src, ALU.mult, ALU.add)); linked()
                    src = r_
                link(dve.tensor_scalar(sin[:], r_, -math.pi + 1e-6, math.pi - 1e-6, ALU.max, ALU.min)); linked()
                link(dve.tensor_scalar(cos[:], sin[:], -1.0, None, ALU.mult)); linked()
                link(dve.tensor_tensor(cos[:], cos[:], sin[:], ALU.min)); linked()
                dve.tensor_scalar(cos[:], cos[:], math.pi / 2, None, ALU.add).then_inc(angles, 1)

            def on_times_gain(n):
                dve.wait_ge(squared, n_squared[0] + 2 * (n + 1))
                dve.wait_ge(fgain_loaded, 16)
                for t in range(NT):
                    v = x[:, t, n * CW:(n + 1) * CW]
                    dve.tensor_tensor(v, v, fgain[:, n * CW:(n + 1) * CW], ALU.mult).then_inc(premultiplied, 1)

            def on_rstd():
                n_squared[0] += 8
                mean(n_squared[0])

            def on_lat_rstd(kind):
                n_squared[0] += 2
                dve.wait_ge(squared, n_squared[0])
                k = ("cq", "ckv").index(kind)
                dve.tensor_scalar(lmean[:, k], lsum[:, k], 1.0 / (512, 256)[k], EPS, ALU.mult, ALU.add).then_inc(lat_mean, 1)

            def on_turn_kr():
                dve.memset(krT[:], 0.0).then_inc(kr_zeroed, 1)

            def on_mix_a(n, g):
                finished(g)
                dve.wait_ge(gates_open, n + 1)
                for t in range(NT):
                    v = gate[:, n, 0, t]
                    dve.tensor_tensor(v, acc[g % 2][t][:], v, ALU.mult).then_inc(acc_taken[g % 2], 1)

            def on_mix_b(n, g):
                finished(g)
                for t in range(NT):
                    v = gate[:, n, 1, t]
                    dve.tensor_tensor(v, acc[g % 2][t][:], v, ALU.mult).then_inc(acc_taken[g % 2], 1)
                dve.wait_ge(acc_taken[g % 2], 2 * (g // 2 + 1))
                for t in range(NT):
                    last = dve.tensor_tensor(stage[:, 0, t], gate[:, n, 0, t], gate[:, n, 1, t], ALU.add)
                last.then_inc(mixed, 1)

            mine = {"evac_kw": on_evac_kw, "headsq": on_headsq, "headscale": on_headscale, "isc": on_isc, "topk": on_topk,
                    "select": on_select, "mask": on_mask, "norm": on_norm, "split_y": on_split_y, "split_x": on_split_x,
                    "split_pool": on_split_pool, "split_lat": on_split_lat, "split_mix": on_split_mix, "res": on_res,
                    "rstd": on_rstd, "lat_rstd": on_lat_rstd, "mix_a": on_mix_a, "turn_kr": on_turn_kr, "mix_b": on_mix_b,
                    "rstd0": on_rstd, "angles": on_angles, "times_gain": on_times_gain}

            def run(n):
                for step_, *args in at.get(n, []):
                    if step_ in mine:
                        mine[step_](*args)

            dve.memset(minus_half[:], -0.5).then_inc(consts_set, 1)
            dve.wait_ge(cols_ready, 1)
            for m in range(KT // 2):
                low([xT_lo[:, 2 * m], xT_lo[:, 2 * m + 1]], [xT_hi[:, 2 * m], xT_hi[:, 2 * m + 1]], (m + 1) % 4, G_ATTN1 + 2 * m)
                if m % 2:
                    split(groups[0][2])
            dve.tensor_tensor(gqk[:], cols[:, G_Q:G_Q + 1], cols[:, G_K:G_K + 1], ALU.mult).then_inc(gqk_ready, 1)

            def convolve(bank, dest, j, base):
                seeds.now += 1
                dve.wait_ge(conv_seeded, seeds.value())
                for tap, back in ((1, 1), (0, 2)):
                    for cc in range(2):
                        k = CONV_COL + base + 2 * (bank % 2) + cc + tap * CT
                        o = dest[:, 2 * (bank % 2) + cc, back:S]
                        last = dve.scalar_tensor_tensor(o, T[bank][:, cc * S:(cc + 1) * S - back],
                                                        cols[:, bass.ds(j * 4 + k, 1)], o, ALU.mult, ALU.add)
                        if tap:
                            link(last)
                    if tap:
                        linked()
                last.then_inc(conv_done, 1)
                convs.now += 1

            def multiply():
                silus.now += 1
                dve.wait_ge(silu_done, silus.value())
                dve.wait_ge(conv_done, convs.value())
                dve.tensor_tensor(half_b, half_a, half_b, ALU.mult).then_inc(hidden, 1)

            def hidden_low(j):
                hiddens.now += 1
                dve.wait_ge(hidden_hi, hiddens.value())
                v = bass.ds(j * 4, 4)
                dve.tensor_tensor(f_lo[:, v], half_b, f_hi[:, v].bitcast(F32), ALU.subtract).then_inc(f_ready, 1)

            def product(par):
                dve.wait_ge(w_used, chunk.value(-LEAD - 1))
                for t in range(NT):
                    sg = half_a.rearrange("p (t a) b -> p t (a b)", t=NT)[:, t]
                    last = dve.scalar_tensor_tensor(stage[:, 0, t], acc[par][t][:], rstd[:, t:t + 1], sg, ALU.mult, ALU.mult)
                    if t == 0:
                        last.then_inc(acc_taken[par], 1)
                last.then_inc(acc_taken[par], 1)

            def product_low(j):
                for b in range(2):
                    splits.now += 1
                    dve.wait_ge(split_hi, splits.value())
                    v = bass.ds(j * 4 + 2 * b, 2)
                    dve.tensor_tensor(f_lo[:, v].rearrange("p a b -> p (a b)"), T[b][:],
                                      f_hi[:, v].rearrange("p a b -> p (a b)").bitcast(F32), ALU.subtract).then_inc(split_lo, 1)

            def feed_forward(layer, g0):
                par = g0 % 2

                def value_steps(j):
                    if layer == 1:
                        return {2: lambda: convolve(2, half_b, j, FT), 3: lambda: convolve(3, half_b, j, FT),
                                4: multiply, 6: lambda: hidden_low(j)}
                    return {0: lambda: product(1 - par), 2: lambda: product_low(j)}

                def pair(j):
                    first_ = isinstance(j, int)
                    steps = {} if first_ else value_steps(j - 1)
                    if layer == 1:
                        steps.update({10: lambda: convolve(0, half_a, j, 0), 11: lambda: convolve(1, half_a, j, 0)})
                    for c in range(2 * KT // KC):
                        split(CW)
                        if first_:
                            run(chunk.now - 1 - LEAD)
                        if c - LEAD in steps:
                            steps[c - LEAD]()
                counts = {"chunk": chunk, "step": step_n, "splits": splits, "convs": convs, "seeds": seeds,
                          "hiddens": hiddens, "silus": silus}
                one = layer == 1
                per = {"chunk": 16, "step": 8 if one else 0, "splits": 0 if one else 2, "convs": 4 if one else 0,
                       "seeds": 4 if one else 0, "hiddens": 1 if one else 0, "silus": 1 if one else 0}
                with_loop(dve, counts, pair, per)
                return value_steps(PAIRS - 1)

            g, steps = 0, {}
            while g < len(groups):
                if g in (G_UP1, G_UP2):
                    steps = feed_forward(1 if g == G_UP1 else 2, g)
                    g += 2 * PAIRS
                    continue
                name, _, width, ks, _ = groups[g]
                for c in range(len(ks)):
                    if chunk.now < first[g] + c + 1:
                        split(width)
                    if chunk.now - 1 - LEAD >= 0:
                        run(first[g] + c - LEAD)
                    if c - LEAD in steps:
                        steps[c - LEAD]()
                steps = {}
                g += 1
            for n in range(n_end - LEAD, n_end + 8):
                run(n)
            dve.wait_ge(rstd_ready, 5)
            dve.wait_ge(premultiplied, 6)
            for t, lo_, hi_ in ((0, 0, 2 * CW), (0, 2 * CW, 3 * CW), (0, 3 * CW, D), (1, 3 * CW, D)):
                v, r = x[:, t, lo_:hi_], rstd[:, t:t + 1]
                if hi_ < D:
                    dve.tensor_scalar(v, v, r, None, ALU.mult).then_inc(normalised, 1)
                else:
                    dve.scalar_tensor_tensor(v, v, r, fgain[:, lo_:hi_], ALU.mult, ALU.mult).then_inc(normalised, 1)


_WHOLE = ["x", "w_in", "pool_w", "w_out", "w_up", "w_down", "positions_2", "final_norm_2"]
_LAYER = ["w_in_2", "w_uq_2", "w_ukv_2", "w_branch_a_2", "w_branch_b_2", "w_out_2", "w_gate_2", "w_up_2", "w_down_2"]
_GAINS = ["attn_norm_g", "ffn_norm_g", "attn_norm_2", "ffn_norm_2", "pool_scale", "q_norm_2", "kv_norm_2", "q_norm_g", "k_norm_g"]


def shape_constants():
    t = np.arange(S)
    causal = np.where(t[None, :] <= t[:, None], np.float32(BIG), np.float32(FMIN)).astype(np.float32)
    pool = np.zeros((P, 4, KEYS), np.float32)
    for w, window in enumerate(WINDOWS):
        inside = (t[:, None] <= t[None, :]) & (t[:, None] > t[None, :] - window)
        m = inside / np.minimum(t + 1, window)[None, :] - np.eye(S)
        pool[:, w, 0:S], pool[:, w, S:] = m[0:P], m[P:, P:]
    freq = np.concatenate([ROPE_THETA ** (-np.arange(0, d, 2) / d) for d in (ROPE_A, ROPE_B)])
    return {"c_ident": np.eye(P, dtype=np.float32),
            "c_causal": np.ascontiguousarray(np.concatenate([causal[0:P, 0:P], causal[P:, :]], axis=1)),
            "c_pool": pool, "c_freq": np.ascontiguousarray(np.broadcast_to(freq.astype(np.float32), (P, 48)))}


def kernel(**inputs):
    import concourse.bacc as bacc
    from concourse.bass_utils import run_bass_kernel_spmd

    nc = bacc.Bacc("TRN2", target_bir_lowering=False, num_devices=1)
    arrays, views = {}, {}
    laid_out = {n: inputs[n] for n in _WHOLE + _LAYER}
    laid_out["gains"] = np.concatenate([np.reshape(inputs[n], (-1, P)) for n in _GAINS])
    laid_out["taps"] = np.concatenate([inputs["conv_w"], np.reshape(inputs["conv_b"], (1, -1))])
    for name, value in (laid_out | shape_constants()).items():
        value = np.ascontiguousarray(value)
        arrays[f"in_{name}"] = value
        view = nc.dram_tensor(f"in_{name}", value.shape, mybir.dt.from_np(value.dtype), kind="ExternalInput").ap()
        views[name] = view[0] if name in _LAYER else view
    out = nc.dram_tensor("out_0", (1, S, D), F32, kind="ExternalOutput").ap()
    two_layer_kernel(nc, views, out)
    result = run_bass_kernel_spmd(nc, [arrays], core_ids=[0])
    return result.results[0]["out_0"]
```
